# Optimizing a Trainium2 kernel written in Bass

```python
import numpy as np
import jax, jax.numpy as jnp
from jax import lax

D_MODEL = 1024
BATCH = 1
SEQ = 256
DEPTH = 2

MEM_LEN = 256
MIX_WIDTH = D_MODEL
NSA_WIDTH = MIX_WIDTH // 2
POOL_WIDTH = MIX_WIDTH - NSA_WIDTH
HEAD_DIM = 64
N_HEADS = NSA_WIDTH // HEAD_DIM
N_KV_HEADS = 2
GROUP = N_HEADS // N_KV_HEADS
KV_WIDTH = N_KV_HEADS * HEAD_DIM
ROPE_DIM = HEAD_DIM // 4
ROPE_THETA = 500000.0
CMP_LEN = 32
CMP_STRIDE = 16
CMP_HIDDEN = 256
SEL_BLOCK = 64
SEL_TOP_N = 16
N_LOCAL_BLOCKS = 2
WINDOW = 512
Q_BLOCK = 128
N_BRANCH = 3
POOL_WINDOWS = (2, 4, 8, 16)
N_POOL_GROUPS = len(POOL_WINDOWS)
POOL_GROUP = POOL_WIDTH // N_POOL_GROUPS
IN_WIDTH = NSA_WIDTH + 6 * KV_WIDTH + N_HEADS * N_BRANCH + POOL_WIDTH
X_HEADS = 4
X_HEAD_DIM = D_MODEL // X_HEADS
D_FF = 2816
N_EXPERTS = 8
TOP_K = 2
D_FF_EXPERT = 3584
N_DENSE = (DEPTH + 1) // 2
N_MOE = DEPTH // 2
EPS = 1e-6

kernel_name = "hybrid_nsa_pool_moe_block"

def rms_norm(x, g):
    xf = x.astype(jnp.float32)
    y = xf * lax.rsqrt(jnp.mean(xf * xf, axis=-1, keepdims=True) + EPS)
    return (y * g.astype(jnp.float32)).astype(x.dtype)

def partial_rope(x, pos):
    half = ROPE_DIM // 2
    inv = ROPE_THETA ** (-jnp.arange(half, dtype=jnp.float32) / half)
    ang = pos.astype(jnp.float32)[:, None] * inv[None, :]
    cos = jnp.cos(ang)[None, :, None, :]
    sin = jnp.sin(ang)[None, :, None, :]
    xr = x[..., :ROPE_DIM].astype(jnp.float32)
    x1, x2 = xr[..., :half], xr[..., half:]
    rot = jnp.concatenate([x1 * cos - x2 * sin, x2 * cos + x1 * sin], axis=-1)
    return jnp.concatenate([rot.astype(x.dtype), x[..., ROPE_DIM:]], axis=-1)

def masked_softmax(logits, mask):
    lf = jnp.where(mask, logits.astype(jnp.float32), -jnp.inf)
    m = jnp.max(lf, axis=-1, keepdims=True)
    m = jnp.where(jnp.isfinite(m), m, 0.0)
    e = jnp.where(mask, jnp.exp(lf - m), 0.0)
    s = jnp.sum(e, axis=-1, keepdims=True)
    return e / jnp.maximum(s, jnp.finfo(jnp.float32).tiny)

def compress_blocks(kv, pe, w1, b1, w2):
    B, S, G, dh = kv.shape
    n_cmp = (S - CMP_LEN) // CMP_STRIDE + 1
    idx = np.arange(n_cmp)[:, None] * CMP_STRIDE + np.arange(CMP_LEN)[None, :]
    blk = kv[:, idx] + pe[None, None, :, None, :]
    blk = jnp.transpose(blk, (0, 1, 3, 2, 4)).reshape(B, n_cmp, G, CMP_LEN * dh)
    hid = jax.nn.gelu(jnp.einsum('bcgf,fh->bcgh', blk, w1) + b1)
    return jnp.einsum('bcgh,hd->bcgd', hid, w2)

def nsa_attention(q, k_cmp_raw, v_cmp_raw, k_slc, v_slc, k_win, v_win, gates,
                  pe_k, w1_k, b1_k, w2_k, pe_v, w1_v, b1_v, w2_v):
    B, S, H, dh = q.shape
    scale = dh ** -0.5
    pos = jnp.arange(S)
    q_rot = partial_rope(q, pos)
    k_slc = partial_rope(k_slc, pos)
    k_win = partial_rope(k_win, pos)
    k_cmp = compress_blocks(k_cmp_raw, pe_k, w1_k, b1_k, w2_k)
    v_cmp = compress_blocks(v_cmp_raw, pe_v, w1_v, b1_v, w2_v)
    n_cmp = k_cmp.shape[1]
    cmp_start = np.arange(n_cmp) * CMP_STRIDE
    cmp_end = jnp.asarray(cmp_start + CMP_LEN - 1)
    n_blk = S // SEL_BLOCK
    n_top = min(SEL_TOP_N, n_blk)
    sel_start = np.arange(n_blk) * SEL_BLOCK
    cover = jnp.asarray(((cmp_start[:, None] < sel_start[None, :] + SEL_BLOCK) &
                         (cmp_start[:, None] + CMP_LEN > sel_start[None, :])).astype(np.float32))
    ks_blocks = jnp.transpose(k_slc.reshape(B, n_blk, SEL_BLOCK, N_KV_HEADS, dh), (0, 3, 1, 2, 4))
    vs_blocks = jnp.transpose(v_slc.reshape(B, n_blk, SEL_BLOCK, N_KV_HEADS, dh), (0, 3, 1, 2, 4))
    pad = ((0, 0), (WINDOW, 0), (0, 0), (0, 0))
    k_win_pad = jnp.pad(k_win, pad)
    v_win_pad = jnp.pad(v_win, pad)
    blk_id = jnp.arange(n_blk)
    b_idx = jnp.arange(B)[:, None, None, None]
    g_idx = jnp.arange(N_KV_HEADS)[None, :, None, None]

    def one_block(qi):
        q0 = qi * Q_BLOCK
        t = q0 + jnp.arange(Q_BLOCK)
        qb = lax.dynamic_slice_in_dim(q, q0, Q_BLOCK, axis=1).reshape(B, Q_BLOCK, N_KV_HEADS, GROUP, dh)
        qrb = lax.dynamic_slice_in_dim(q_rot, q0, Q_BLOCK, axis=1).reshape(B, Q_BLOCK, N_KV_HEADS, GROUP, dh)
        lc = jnp.einsum('bqgrd,bcgd->bgrqc', qb, k_cmp) * scale
        pc = masked_softmax(lc, cmp_end[None, :] <= t[:, None])
        oc = jnp.einsum('bgrqc,bcgd->bqgrd', pc.astype(v_cmp.dtype), v_cmp)
        imp = jnp.einsum('bgrqc,cn->bgqn', pc, cover)
        tb = t // SEL_BLOCK
        future = blk_id[None, :] > tb[:, None]
        dist = tb[:, None] - blk_id[None, :]
        forced = (blk_id[None, :] == 0) | ((dist >= 0) & (dist < N_LOCAL_BLOCKS))
        score = jnp.where(future, -jnp.inf, jnp.where(forced, jnp.inf, imp))
        _, sel = lax.top_k(score, n_top)
        ksel = ks_blocks[b_idx, g_idx, sel].reshape(B, N_KV_HEADS, Q_BLOCK, n_top * SEL_BLOCK, dh)
        vsel = vs_blocks[b_idx, g_idx, sel].reshape(B, N_KV_HEADS, Q_BLOCK, n_top * SEL_BLOCK, dh)
        kpos = (sel[..., None] * SEL_BLOCK + jnp.arange(SEL_BLOCK)).reshape(B, N_KV_HEADS, Q_BLOCK, n_top * SEL_BLOCK)
        ls = jnp.einsum('bqgrd,bgqkd->bgrqk', qrb, ksel) * scale
        ps = masked_softmax(ls, (kpos <= t[None, None, :, None])[:, :, None])
        osl = jnp.einsum('bgrqk,bgqkd->bqgrd', ps.astype(vsel.dtype), vsel)
        kw = lax.dynamic_slice_in_dim(k_win_pad, q0, Q_BLOCK + WINDOW, axis=1)
        vw = lax.dynamic_slice_in_dim(v_win_pad, q0, Q_BLOCK + WINDOW, axis=1)
        wpos = q0 - WINDOW + jnp.arange(Q_BLOCK + WINDOW)
        diff = t[:, None] - wpos[None, :]
        mw = (diff >= 0) & (diff < WINDOW) & (wpos[None, :] >= 0)
        lw = jnp.einsum('bqgrd,bkgd->bgrqk', qrb, kw) * scale
        pw = masked_softmax(lw, mw)
        ow = jnp.einsum('bgrqk,bkgd->bqgrd', pw.astype(vw.dtype), vw)
        gb = lax.dynamic_slice_in_dim(gates, q0, Q_BLOCK, axis=1).reshape(B, Q_BLOCK, N_KV_HEADS, GROUP, N_BRANCH)
        o = gb[..., 0:1] * oc + gb[..., 1:2] * osl + gb[..., 2:3] * ow
        return o.reshape(B, Q_BLOCK, H * dh)

    out = lax.map(one_block, jnp.arange(S // Q_BLOCK))
    return jnp.transpose(out, (1, 0, 2, 3)).reshape(B, S, H * dh)

def pool_mixer(u, w_pool, pool_scale):
    B, S, _ = u.shape
    ug = u.reshape(B, S, N_POOL_GROUPS, POOL_GROUP).astype(jnp.float32)
    c = jnp.pad(jnp.cumsum(ug, axis=1), ((0, 0), (1, 0), (0, 0), (0, 0)))
    outs = []
    for g, w in enumerate(POOL_WINDOWS):
        cg = c[:, :, g]
        hi = cg[:, 1:]
        lo = jnp.pad(cg[:, :S + 1 - w], ((0, 0), (w - 1, 0), (0, 0)))
        cnt = jnp.minimum(jnp.arange(1, S + 1), w).astype(jnp.float32)[None, :, None]
        outs.append((hi - lo) / cnt - ug[:, :, g])
    d = jnp.stack(outs, axis=2).astype(u.dtype)
    y = jnp.einsum('bsgc,gce->bsge', d, w_pool).reshape(B, S, POOL_WIDTH)
    return y * pool_scale

def hybrid_mixer(h, w_in, pe_k, w1_k, b1_k, w2_k, pe_v, w1_v, b1_v, w2_v, w_pool, pool_scale, w_out):
    B, S, _ = h.shape
    z = h @ w_in
    o1 = NSA_WIDTH
    o2 = o1 + 6 * KV_WIDTH
    o3 = o2 + N_HEADS * N_BRANCH
    q = z[..., :o1].reshape(B, S, N_HEADS, HEAD_DIM)
    kv = z[..., o1:o2].reshape(B, S, 6, N_KV_HEADS, HEAD_DIM)
    gates = jax.nn.sigmoid(z[..., o2:o3]).reshape(B, S, N_HEADS, N_BRANCH)
    u = z[..., o3:]
    a = nsa_attention(q, kv[:, :, 0], kv[:, :, 1], kv[:, :, 2], kv[:, :, 3], kv[:, :, 4], kv[:, :, 5], gates,
                      pe_k, w1_k, b1_k, w2_k, pe_v, w1_v, b1_v, w2_v)
    p = pool_mixer(u, w_pool, pool_scale)
    return jnp.concatenate([a, p], axis=-1) @ w_out

def memory_cross_attention(h, m, wq, wk, wv, wo):
    B, S, _ = h.shape
    M = m.shape[1]
    q = (h @ wq).reshape(B, S, X_HEADS, X_HEAD_DIM)
    k = (m @ wk).reshape(B, M, X_HEADS, X_HEAD_DIM)
    v = (m @ wv).reshape(B, M, X_HEADS, X_HEAD_DIM)
    logits = jnp.einsum('bshd,bmhd->bhsm', q, k).astype(jnp.float32) * (X_HEAD_DIM ** -0.5)
    p = jax.nn.softmax(logits, axis=-1).astype(v.dtype)
    o = jnp.einsum('bhsm,bmhd->bshd', p, v).reshape(B, S, X_HEADS * X_HEAD_DIM)
    return o @ wo

def swiglu(h, wg, wu, wd):
    return (jax.nn.silu(h @ wg) * (h @ wu)) @ wd

def moe_swiglu(h, w_router, wg, wu, wd):
    logits = (h @ w_router).astype(jnp.float32)
    top_v, top_i = lax.top_k(logits, TOP_K)
    gate = jax.nn.softmax(top_v, axis=-1)
    comb = jnp.sum(jax.nn.one_hot(top_i, N_EXPERTS, dtype=jnp.float32) * gate[..., None], axis=-2)
    out = jnp.zeros_like(h)
    for e in range(N_EXPERTS):
        out = out + comb[..., e:e + 1].astype(h.dtype) * swiglu(h, wg[e], wu[e], wd[e])
    return out

def setup_inputs(seed: int = 0) -> dict:
    key = jax.random.key(seed)
    ks = iter(jax.random.split(key, 40))

    def nrm(shape, std):
        return jax.random.normal(next(ks), shape, jnp.float32) * std

    def gain(shape):
        return 1.0 + nrm(shape, 0.02)

    L = DEPTH
    return {
        "x": nrm((BATCH, SEQ, D_MODEL), 1.0),
        "mem": nrm((BATCH, MEM_LEN, D_MODEL), 1.0),
        "norm_mix": gain((L, D_MODEL)),
        "w_in": nrm((L, D_MODEL, IN_WIDTH), D_MODEL ** -0.5),
        "cmp_pe_k": nrm((L, CMP_LEN, HEAD_DIM), 0.02),
        "cmp_w1_k": nrm((L, CMP_LEN * HEAD_DIM, CMP_HIDDEN), (CMP_LEN * HEAD_DIM) ** -0.5),
        "cmp_b1_k": nrm((L, CMP_HIDDEN), 0.02),
        "cmp_w2_k": nrm((L, CMP_HIDDEN, HEAD_DIM), CMP_HIDDEN ** -0.5),
        "cmp_pe_v": nrm((L, CMP_LEN, HEAD_DIM), 0.02),
        "cmp_w1_v": nrm((L, CMP_LEN * HEAD_DIM, CMP_HIDDEN), (CMP_LEN * HEAD_DIM) ** -0.5),
        "cmp_b1_v": nrm((L, CMP_HIDDEN), 0.02),
        "cmp_w2_v": nrm((L, CMP_HIDDEN, HEAD_DIM), CMP_HIDDEN ** -0.5),
        "w_pool": nrm((L, N_POOL_GROUPS, POOL_GROUP, POOL_GROUP), POOL_GROUP ** -0.5),
        "pool_scale": gain((L, POOL_WIDTH)),
        "w_out": nrm((L, MIX_WIDTH, D_MODEL), MIX_WIDTH ** -0.5),
        "norm_x": gain((L, D_MODEL)),
        "norm_mem": gain((L, D_MODEL)),
        "wq_x": nrm((L, D_MODEL, X_HEADS * X_HEAD_DIM), D_MODEL ** -0.5),
        "wk_x": nrm((L, D_MODEL, X_HEADS * X_HEAD_DIM), D_MODEL ** -0.5),
        "wv_x": nrm((L, D_MODEL, X_HEADS * X_HEAD_DIM), D_MODEL ** -0.5),
        "wo_x": nrm((L, X_HEADS * X_HEAD_DIM, D_MODEL), D_MODEL ** -0.5),
        "norm_ffn": gain((L, D_MODEL)),
        "ffn_wg": nrm((N_DENSE, D_MODEL, D_FF), D_MODEL ** -0.5),
        "ffn_wu": nrm((N_DENSE, D_MODEL, D_FF), D_MODEL ** -0.5),
        "ffn_wd": nrm((N_DENSE, D_FF, D_MODEL), D_FF ** -0.5),
        "moe_router": nrm((N_MOE, D_MODEL, N_EXPERTS), D_MODEL ** -0.5),
        "moe_wg": nrm((N_MOE, N_EXPERTS, D_MODEL, D_FF_EXPERT), D_MODEL ** -0.5),
        "moe_wu": nrm((N_MOE, N_EXPERTS, D_MODEL, D_FF_EXPERT), D_MODEL ** -0.5),
        "moe_wd": nrm((N_MOE, N_EXPERTS, D_FF_EXPERT, D_MODEL), D_FF_EXPERT ** -0.5),
        "norm_final": gain((D_MODEL,)),
    }

def reference(x, mem, norm_mix, w_in, cmp_pe_k, cmp_w1_k, cmp_b1_k, cmp_w2_k,
              cmp_pe_v, cmp_w1_v, cmp_b1_v, cmp_w2_v, w_pool, pool_scale, w_out,
              norm_x, norm_mem, wq_x, wk_x, wv_x, wo_x, norm_ffn,
              ffn_wg, ffn_wu, ffn_wd, moe_router, moe_wg, moe_wu, moe_wd, norm_final):
    for layer in range(DEPTH):
        h = rms_norm(x, norm_mix[layer])
        x = x + hybrid_mixer(h, w_in[layer],
                             cmp_pe_k[layer], cmp_w1_k[layer], cmp_b1_k[layer], cmp_w2_k[layer],
                             cmp_pe_v[layer], cmp_w1_v[layer], cmp_b1_v[layer], cmp_w2_v[layer],
                             w_pool[layer], pool_scale[layer], w_out[layer])
        h = rms_norm(x, norm_x[layer])
        m = rms_norm(mem, norm_mem[layer])
        x = x + memory_cross_attention(h, m, wq_x[layer], wk_x[layer], wv_x[layer], wo_x[layer])
        h = rms_norm(x, norm_ffn[layer])
        j = layer // 2
        if layer % 2 == 0:
            x = x + swiglu(h, ffn_wg[j], ffn_wu[j], ffn_wd[j])
        else:
            x = x + moe_swiglu(h, moe_router[j], moe_wg[j], moe_wu[j], moe_wd[j])
    return rms_norm(x, norm_final)


_drawn_inputs = setup_inputs


def setup_inputs(seed=0):
    import zlib

    import numpy as np

    out = dict(_drawn_inputs(seed))
    spreads = {}
    factors = {'cmp_pe_k': 8.0,
     'cmp_b1_k': 8.0,
     'cmp_pe_v': 8.0,
     'cmp_b1_v': 4.656,
     'norm_x': 8.0,
     'norm_mem': 5.194,
     'norm_final': 8.59,
     'norm_ffn': 3.427}
    for name, (base, spread) in spreads.items():
        noise = np.random.default_rng([zlib.crc32(name.encode()), seed]).standard_normal(out[name].shape)
        drawn = base * np.exp(spread * noise) if base else spread * noise
        out[name] = __import__('jax').numpy.asarray(drawn.astype(out[name].dtype))
    for name, factor in factors.items():
        out[name] = (out[name] * factor).astype(out[name].dtype)
    return out
```

```python
from contextlib import ExitStack

import numpy as np

import concourse.bass as bass
from concourse import mybir

F32 = mybir.dt.float32
F32R = mybir.dt.float32r
BF16 = mybir.dt.bfloat16
I32 = mybir.dt.int32
ALU = mybir.AluOpType
ACT = mybir.ActivationFunctionType
AX = mybir.AxisListType.X

P = 128
DEPTH, SEQ, D = 2, 256, 1024
NT = SEQ // P
KD = D // P
HEADS, HD, GRP = 8, 64, 4
NSA_W, POOL_W, IN_W = 512, 512, 1816
CMP_LEN, CMP_STRIDE, N_CMP = 32, 16, 15
CMP_J = CMP_LEN * HD // P
ROPE = 16
XH = 4
FF_STEP, FF_STEPS = 256, 11
E, MOE_STEP, MOE_STEPS = 8, 512, 7
CAP = 128
NCOL = 17
ZW = IN_W // 4
EPS = 1e-6
NEG = -1e30

Z_KSLC, Z_KWIN, Z_KCMP, Z_VCMP, Z_VSLC, Z_VWIN, Z_GATE, Z_U = 512, 640, 768, 896, 1024, 1152, 1280, 1304

SMALL = {}
_o = 0
for _n, _w in (("g_mix", 8), ("g_mem", 8), ("g_x", 8), ("g_ffn", 8), ("pool_scale", 4), ("b1", 4), ("pe", 32),
               ("w2k", 128), ("w2v", 128), ("w_pool", 512)):
    SMALL[_n] = (_o, _w)
    _o += _w
SMALL_W = _o
CONST = {}
_o = 0
for _n, _w in (("ident", 128), ("below", 128), ("iota", 128), ("jlt", 64), ("cos", 32), ("sin", 32),
               ("cmp_mask", 128), ("band", 4 * 384), ("causal", 256)):
    CONST[_n] = (_o, _w)
    _o += _w
CONST_W = _o
CONST_KEEP = CONST["causal"][0]

LAYER_SPLITS = 7
LAYER_LOADS = 8
PER_LAYER_SPLITS = LAYER_SPLITS + FF_STEPS
PER_LAYER_LOADS = LAYER_LOADS + FF_STEPS
MOE_SPLITS = (2 * LAYER_SPLITS + FF_STEPS,) * 2 + (FF_STEPS,)
MOE_LOADS = (2 * LAYER_LOADS + FF_STEPS,) * 2 + (FF_STEPS,)


def build(nc, x_d, mem_d, wl_d, wf_d, wm_d, small_d, const_d, router_d, gfin_d, out_d):
    ctx = ExitStack()
    with ctx:
        base = 16512

        def at(name, off, shape, dt=F32):
            return nc.alloc_sbuf_tensor_at(name, [P] + shape, dt, offset=base + off)

        def sem(name):
            return ctx.enter_context(nc.semaphore(name))

        K = 1024
        x = at("x", 0, [NT, D])
        xs = at("xs", 8 * K, [NT, D])
        hiA, loA = at("hiA", 16 * K, [KD, SEQ], F32R), at("loA", 24 * K, [KD, SEQ], F32R)
        hiB, loB = at("hiB", 32 * K, [KD, SEQ], F32R), at("loB", 40 * K, [KD, SEQ], F32R)
        stage = [at(f"stage{i}", 48 * K + (i * 48 if i < 2 else 96) * K, [4096]) for i in range(3)]
        whi = [at(f"whi{i}", 64 * K + (i * 48 if i < 2 else 96) * K, [4096], F32R) for i in range(3)]
        wlo = [at(f"wlo{i}", 80 * K + (i * 48 if i < 2 else 96) * K, [4096], F32R) for i in range(3)]
        T = 144 * K
        z = at("z", T, [NT, IN_W])
        qk_rot = at("qk_rot", T + 14592, [NT, 768])
        q_raw_T = at("q_raw_T", T + 20736, [4, SEQ])
        q_rot_T = at("q_rot_T", T + 24832, [4, SEQ])
        k_T = at("k_T", T + 28928, [2, SEQ])
        probs = [at("probs0", T + 30976, [2048]), at("probs1", T + 39168, [2048])]
        rope_c = at("rope_c", T + 30976, [NT, 12, ROPE])
        rope_s = at("rope_s", T + 30976 + 1536, [NT, 12, ROPE])
        blk_T = at("blk_T", T + 39168, [2, CMP_J, 2 * N_CMP])
        d_T = at("d_T", T + 39168 + 3840, [4, SEQ])
        pt = [at(f"pt{i}", T + 14592 + 2048 * i, [512]) for i in range(2)]
        o_tok = at("o_tok", T + 30976 + 4096, [NT, NSA_W])
        cmask_f = at("cmask_f", T + 39168, [256])
        kx_T, v_x, q_x_T = at("kx_T", T, [8, SEQ]), at("v_x", T + 8 * K, [NT, D]), at("q_x_T", T + 16 * K, [8, SEQ])
        p_x = at("p_x", T + 24 * K, [NT, XH, SEQ])
        pt_x = at("pt_x", T + 32 * K, [NT, XH, SEQ])
        C = 192 * K
        small = at("small", C, [SMALL_W])
        const = at("const", C + 3360, [CONST_KEEP])
        o = C + 3360 + 4 * CONST_KEEP
        router = at("router", o, [KD, E]); o += 256
        ident_bf = at("ident_bf", o, [P], BF16); o += 256
        causal_bf = at("causal_bf", o, [256], BF16); o += 512
        stat = at("stat", o, [80]); o += 320
        gates = at("gates", o, [NT, 24]); o += 192
        k_cmp_T = at("k_cmp_T", o, [16]); o += 64
        v_bd = at("v_bd", o, [2, 256]); o += 2048
        hid = at("hid", T + 48384, [2, 2, 2 * N_CMP])
        MOE = 32 * K
        hid_tok = at("hid_tok", MOE, [2, MOE_STEP])
        a_hi, a_lo = at("a_hi", MOE + 4096, [512], F32R), at("a_lo", MOE + 6144, [512], F32R)
        down_out = at("down_out", MOE + 8192, [D])
        onehot = at("onehot", MOE + 12288, [NT, CAP])
        onehot_g = at("onehot_g", MOE + 13312, [NT, CAP])
        onehot_gT = at("onehot_gT", MOE + 14336, [SEQ])
        f_sil, f_act = at("f_sil", 16 * K, [512]), at("f_act", 18 * K, [512])
        f_hi, f_lo = at("f_hi", 20 * K, [2, SEQ], F32R), at("f_lo", 22 * K, [2, SEQ], F32R)
        e_hi, e_lo = at("e_hi", 16 * K, [KD, CAP], F32R), at("e_lo", 20 * K, [KD, CAP], F32R)
        p_cmp = at("p_cmp", T + 18688, [16, 32])
        l_cmp = at("l_cmp", T + 47360, [16, 16])
        rt = at("rt", 24 * K, [1024])
        keys = at("keys", 28 * K, [NT, NCOL])
        combs = at("combs", 28 * K + 256, [NT, NCOL])
        items_i = at("items_i", 28 * K + 512, [NCOL + 1], I32)
        items_f = at("items_f", 28 * K + 640, [NCOL + 1])
        ones = at("ones", 29 * K, [P])
        gfin = at("gfin", MOE, [D])
        junk = at("junk", T + 35072, [NT, D], BF16)
        assert base + o <= 229344, o

        PS = ctx.enter_context(nc.psum_tensor("PS", [P, 8, 512], F32))

        def bank(i):
            return PS[:, i, :]

        def cst(n, a=0, b=None):
            off, w = CONST[n]
            return const[:, off + a:off + (w if b is None else b)]

        def sml(n, a=0, b=None):
            off, w = SMALL[n]
            return small[:, off + a:off + (w if b is None else b)]

        ident = cst("ident")
        f32 = lambda ap: ap.bitcast(F32)

        x_in, const_in, small_in, mem_in = sem("x_in"), sem("const_in"), sem("small_in"), sem("mem_in")
        mask_in, gfin_in, out_done = sem("mask_in"), sem("gfin_in"), sem("out_done")
        consts_ready = sem("consts_ready")
        w_in_ring = [sem(f"w_landed{i}") for i in range(3)]
        w_hi = [sem(f"w_hi{i}") for i in range(3)]
        w_lo = [sem(f"w_lo{i}") for i in range(3)]
        w_used = [sem(f"w_used{i}") for i in range(3)]
        x_ready = sem("x_ready")
        ssq_done, ms_done, rstd_done, xs_ready = sem("ssq_done"), sem("ms_done"), sem("rstd_done"), sem("xs_ready")
        xT_done, n_hi, n_lo = sem("xT_done"), sem("n_hi"), sem("n_lo")
        z_done, z_act, z_dve = sem("z_done"), sem("z_act"), sem("z_dve")
        qk_copied, rope_done, rope_part = sem("qk_copied"), sem("rope_done"), sem("rope_part")
        tq_done, xt_done, tr_done, pd_done = sem("tq_done"), sem("xt_done"), sem("tr_done"), sem("pd_done")
        q_rot_ready, q_raw_ready, d_ready = sem("q_rot_ready"), sem("q_raw_ready"), sem("d_ready")
        blk_ready, hid_done, gelu_done = sem("blk_ready"), sem("hid_done"), sem("gelu_done")
        y_done, y_hi, y_lo = sem("y_done"), sem("y_hi"), sem("y_lo")
        kcvc_done, kcvc_ready, cs_done = sem("kcvc_done"), sem("kcvc_ready"), sem("cs_done")
        gate_e, gate_v = sem("gate_e"), sem("gate_v")
        cmp_v, cmp_e, pc_ready, p_cmp_zero = sem("cmp_v"), sem("cmp_e"), sem("pc_ready"), sem("p_cmp_zero")
        s_done, max_done, nm_ready, exps_done, r_done, p_ready = (sem("s_done"), sem("max_done"), sem("nm_ready"),
                                                                  sem("exps_done"), sem("r_done"), sem("p_ready"))
        t_done, pt_act, pt_dve, pv_done = sem("t_done"), sem("pt_act"), sem("pt_dve"), sem("pv_done")
        o_ready, oT_done, cc_hi, cc_lo = sem("o_ready"), sem("oT_done"), sem("cc_hi"), sem("cc_lo")
        mix_out, mix_add = sem("mix_out"), sem("mix_add")
        kvq_done, kvq_act, kvq_dve = sem("kvq_done"), sem("kvq_act"), sem("kvq_dve")
        xs_done, xmax_done, xnm_ready, xexp_done, xr_done, xp_ready = (sem("xs_done"), sem("xmax_done"), sem("xnm_ready"),
                                                                       sem("xexp_done"), sem("xr_done"), sem("xp_ready"))
        xt2_done, pt2_ready = sem("xt2_done"), sem("pt2_ready")
        ox_done, ox_hi, ox_lo, cross_out = sem("ox_done"), sem("ox_hi"), sem("ox_lo"), sem("cross_out")
        f_silu, f_mul, f_hi_s, f_lo_s = sem("f_silu"), sem("f_mul"), sem("f_hi_s"), sem("f_lo_s")
        lg_done, rv, r_exp, pos_done, keys_ready, items_ready = (sem("lg_done"), sem("rv"), sem("r_exp"), sem("pos_done"),
                                                                 sem("keys_ready"), sem("items_ready"))
        oh_ready, oh_g_ready, gath_done, e_hi_s, e_lo_s = (sem("oh_ready"), sem("oh_g_ready"), sem("gath_done"),
                                                           sem("e_hi_s"), sem("e_lo_s"))
        m_silu, m_mul, mt_done, ma_hi, ma_lo = sem("m_silu"), sem("m_mul"), sem("mt_done"), sem("ma_hi"), sem("ma_lo")
        md_ev, ohT_done, ohT_ready, sc_done, sc_add = (sem("md_ev"), sem("ohT_done"),
                                                                sem("ohT_ready"), sem("sc_done"), sem("sc_add"))
        fin_ready = sem("fin_ready")

        block = ctx.enter_context(nc.Block())

        @block.sync
        def _(sp):
            sp.dma_start(x[:], x_d.rearrange("(t p) d -> p t d", p=P)).then_inc(x_in, 16)

            with sp.Fori(0, DEPTH) as l:
                for i in range(16):
                    slot = i % 2
                    if i - 2 in (4, 5):
                        sp.wait_ge(hid_done, l * 2 + (i - 2 - 3))
                    elif i >= 2:
                        split = i - 2 if i - 2 < 4 else i - 4
                        sp.wait_ge(w_lo[slot], l * PER_LAYER_SPLITS + (split // 2 + 1))
                    n = KD * ZW if i < 4 else 4096
                    sp.dma_start(stage[slot][:, 0:n], wl_d[bass.ds(l, 1), i, :, 0:n].rearrange("o p n -> p (o n)")) \
                        .then_inc(w_in_ring[slot], 16)
                with sp.If(l < 1):
                    def load(t, kind):
                        sp.dma_start(stage[kind][:, 0:2048], wf_d[bass.ds(t, 1), kind, :, :].rearrange("o p n -> p (o n)")) \
                            .then_inc(w_in_ring[kind], 16)

                    sp.wait_ge(w_lo[0], LAYER_SPLITS)
                    load(0, 0)
                    sp.wait_ge(w_lo[1], LAYER_SPLITS)
                    load(0, 1)
                    sp.wait_ge(w_lo[0], LAYER_SPLITS + 1)
                    load(1, 0)
                    sp.wait_ge(ox_done, 4)
                    load(0, 2)
                    sp.wait_ge(w_lo[1], LAYER_SPLITS + 1)
                    load(1, 1)
                    with sp.Fori(1, FF_STEPS - 1) as t:
                        sp.wait_ge(w_lo[0], t + (LAYER_SPLITS + 1))
                        load(t + 1, 0)
                        sp.wait_ge(w_lo[2], t + 0)
                        load(t, 2)
                        sp.wait_ge(w_lo[1], t + (LAYER_SPLITS + 1))
                        load(t + 1, 1)
                    sp.wait_ge(w_lo[2], FF_STEPS - 1)
                    load(FF_STEPS - 1, 2)
                    for slot in range(2):
                        sp.wait_ge(w_lo[slot], LAYER_SPLITS + FF_STEPS)

            def load_e(e, s, kind):
                sp.dma_start(stage[kind][:], wm_d[bass.ds(e, 1), s, kind, :, :].rearrange("o p n -> p (o n)")) \
                    .then_inc(w_in_ring[kind], 16)

            def load_item(it, e, e_before, first=False):
                for s in range(MOE_STEPS):
                    n = it * MOE_STEPS + s
                    sp.wait_ge(w_lo[0], n + MOE_SPLITS[0])
                    load_e(e, s, 0)
                    sp.wait_ge(w_lo[1], n + MOE_SPLITS[1])
                    load_e(e, s, 1)
                    if first and s == 0:
                        continue
                    if first and s == 1:
                        sp.wait_ge(ox_done, 4 * DEPTH)
                    sp.wait_ge(w_lo[2], n + (MOE_SPLITS[2] - 1))
                    load_e(e if s else e_before, (s - 1) % MOE_STEPS, 2)

            load_item(0, 0, 0, first=True)
            with sp.Fori(1, E) as it:
                load_item(it, it, it - 1)
            sp.wait_ge(items_ready, 1)
            n_items = sp.value_load(items_i[0:1, NCOL:NCOL + 1], min_val=E, max_val=2 * E)
            with sp.If(n_items > E):
                with sp.Fori(E, n_items) as it:
                    e = sp.value_load(items_i[0:1, bass.ds(it, 1)], min_val=0, max_val=E - 1)
                    eb = sp.value_load(items_i[0:1, bass.ds(it - 1, 1)], min_val=0, max_val=E - 1)
                    load_item(it, e, eb)
            last = sp.value_load(items_i[0:1, bass.ds(n_items - 1, 1)], min_val=0, max_val=E - 1)
            sp.wait_ge(w_lo[2], n_items * MOE_STEPS + (MOE_SPLITS[2] - 1))
            load_e(last, MOE_STEPS - 1, 2)
            for t in range(NT):
                sp.wait_ge(fin_ready, t + 1)
                sp.dma_start(out_d[t * P:(t + 1) * P, :], xs[:, t, :]).then_inc(out_done, 16)
            sp.wait_ge(out_done, 16 * NT)

        @block.gpsimd
        def _(pool):
            pool.dma_start(const[:], const_d[:, 0:CONST_KEEP]).then_inc(const_in, 16)
            pool.dma_start(cmask_f[:], const_d[:, CONST_KEEP:CONST_W]).then_inc(mask_in, 16)
            pool.dma_start(small[:], small_d[0]).then_inc(small_in, 16)
            pool.dma_start(router[:].rearrange("p k e -> p (k e)"), router_d).then_inc(const_in, 16)
            pool.memset(stat[:, 2:4], -0.5).then_inc(consts_ready, 1)
            pool.memset(v_bd[:], 0.0).then_inc(consts_ready, 1)
            pool.wait_ge(consts_ready, 2)

            def rstd(n):
                pool.wait_ge(ms_done, n)
                nc.gpsimd.tensor_tensor(stat[:, 6:8], stat[:, 4:6], stat[:, 2:4], ALU.pow).then_inc(rstd_done, 1)

            for l in range(DEPTH):
                rstd(l * 4 + 1)
                pool.wait_ge(xT_done, l * 16 + 4)
                pool.dma_start(xs[:], mem_d.rearrange("(t p) d -> p t d", p=P)).then_inc(mem_in, 16)
                rstd(l * 4 + 2)
                pool.wait_ge(tq_done, l * 3 + 3)
                pool.memset(p_cmp[:], 0.0).then_inc(p_cmp_zero, 1)
                rstd(l * 4 + 3)
                rstd(l * 4 + 4)
                if l < DEPTH - 1:
                    pool.wait_ge(n_hi, (l + 1) * 16)
                    pool.wait_ge(n_lo, (l + 1) * 16)
                    pool.dma_start(small[:], small_d[l + 1]).then_inc(small_in, 16)
            rstd(DEPTH * 4 + 1)
            pool.dma_start(gfin[:], gfin_d.partition_broadcast(P)).then_inc(gfin_in, 16)
            pool.wait_ge(gfin_in, 16)

        @block.scalar
        def _(act):
            def hi(slot, loads, n=4096):
                act.wait_ge(w_in_ring[slot], loads * 16)
                nc.scalar.activation(whi[slot][:, 0:n], stage[slot][:, 0:n], ACT.Copy).then_inc(w_hi[slot], 1)

            def squares(src):
                for t in range(NT):
                    ins = nc.scalar.activation(junk[:, t, :], src[:, t, :], ACT.Square, accum_out=stat[:, t:t + 1])
                ins.then_inc(ssq_done, 1)

            def norm_hi(l, j, gain, dst):
                for i in range(4):
                    act.wait_ge(xT_done, l * 16 + (4 * j + i + 1))
                    for k in (2 * i, 2 * i + 1):
                        ins = nc.scalar.activation(dst[:, k, :], bank(i)[:, (k % 2) * 256:(k % 2) * 256 + 256], ACT.Copy,
                                                   scale=sml(gain, k, k + 1))
                    ins.then_inc(n_hi, 1)

            def hi_layer(l, s):
                slot, i = s % 2, (s if s < 4 else s + 2)
                if 2 <= s < 6:
                    act.wait_ge(z_done, l * 8 + 2 * (s - 1))
                elif 6 <= s < 8:
                    act.wait_ge(mix_out, l * 4 + 2 * (s - 5))
                elif s >= 8:
                    act.wait_ge(kvq_done, l * 12 + 2 * (s - 7))
                hi(slot, l * PER_LAYER_LOADS + (i // 2 + 1), KD * ZW if s < 4 else 4096)

            def exps(l, u, tt, slot):
                nk = P * (tt + 1)
                act.wait_ge(nm_ready, l * 4 + (u + 1))
                b0 = 2 if u == 3 else 0
                sc = PS[:, b0:b0 + HEADS * nk // 512, :].rearrange("p b n -> p (b n)")
                for h in range(HEADS):
                    ins = nc.scalar.activation(probs[slot][:, h * nk:(h + 1) * nk], sc[:, h * nk:(h + 1) * nk], ACT.Exp,
                                               bias=stat[:, 16 + 8 * slot + h:17 + 8 * slot + h], scale=HD ** -0.5,
                                               accum_out=stat[:, 32 + 8 * slot + h:33 + 8 * slot + h])
                ins.then_inc(exps_done, 1)

            def pt_even(l, i):
                act.wait_ge(t_done, l * 13 + (i + 1))
                if i >= 2:
                    act.wait_ge(pv_done, l * 13 + (i - 1))
                nc.scalar.activation(pt[0][:], bank(6), ACT.Copy).then_inc(pt_act, 1)

            act.wait_ge(x_in, 16)
            act.wait_ge(const_in, 32)
            with act.Fori(0, DEPTH) as l:
                act.wait_ge(x_ready, l * 3 + 1)
                squares(x)
                hi_layer(l, 0)
                act.wait_ge(small_in, l * 16 + 16)
                norm_hi(l, 0, "g_mix", hiA)
                hi_layer(l, 1)
                for c in range(4):
                    act.wait_ge(z_done, l * 8 + (2 * c + 1))
                    nc.scalar.activation(z[:, 0, c * ZW:(c + 1) * ZW], bank(4 + 2 * (c % 2))[:, 0:ZW], ACT.Copy).then_inc(z_act, 1)
                    if c == 1:
                        act.wait_ge(z_act, l * 4 + 2)
                        act.wait_ge(z_dve, l * 4 + 2)
                        nc.scalar.activation(qk_rot[:], z[:, :, 0:768], ACT.Copy).then_inc(qk_copied, 1)
                    if c < 2:
                        hi_layer(l, c + 2)
                    if c == 2:
                        act.wait_ge(mem_in, l * 16 + 16)
                        act.wait_ge(ms_done, l * 4 + 1)
                        squares(xs)
                norm_hi(l, 1, "g_mem", hiA)
                act.wait_ge(z_dve, l * 4 + 4)
                act.wait_ge(z_act, l * 4 + 4)
                nc.scalar.activation(gates[:], z[:, :, Z_GATE:Z_GATE + 24], ACT.Exp, scale=-1.0).then_inc(gate_e, 1)
                act.wait_ge(tq_done, l * 3 + 1)
                nc.scalar.activation(q_rot_T[:, 0:2, :], bank(4).rearrange("p (c t) -> p c t", c=2), ACT.Copy).then_inc(q_rot_ready, 1)
                act.wait_ge(tq_done, l * 3 + 3)
                nc.scalar.activation(k_T[:], bank(6).rearrange("p (c t) -> p c t", c=2), ACT.Copy).then_inc(q_rot_ready, 1)
                act.wait_ge(tr_done, l * 2 + 1)
                nc.scalar.activation(q_raw_T[:, 0:2, :], bank(0).rearrange("p (c t) -> p c t", c=2), ACT.Copy).then_inc(q_raw_ready, 1)
                act.wait_ge(pd_done, l * 2 + 1)
                nc.scalar.activation(d_T[:, 0:2, :], bank(2).rearrange("p (c t) -> p c t", c=2), ACT.Copy).then_inc(d_ready, 1)
                hi_layer(l, 4)
                hi_layer(l, 5)
                exps(l, 0, 1, 0)
                for kv in range(2):
                    act.wait_ge(hid_done, l * 2 + (kv + 1))
                    for hc in range(2):
                        g = (kv * 2 + hc)
                        ins = nc.scalar.activation(hid[:, kv, hc, :], bank(6)[:, g * 32:g * 32 + 2 * N_CMP], ACT.Gelu_apprx_tanh,
                                                   bias=sml("b1", g, g + 1))
                    ins.then_inc(gelu_done, 1)
                for i in range(2):
                    act.wait_ge(y_done, l * 2 + (i + 1))
                    for g in (2 * i, 2 * i + 1):
                        ins = nc.scalar.activation(hiB[:, 4 + g, :], bank(4 + i)[:, (g % 2) * 256:(g % 2) * 256 + 256], ACT.Copy,
                                                   scale=sml("pool_scale", g, g + 1))
                    ins.then_inc(y_hi, 1)
                act.wait_ge(cmp_v, l * 8 + 5)
                nc.scalar.activation(l_cmp[:], l_cmp[:], ACT.Exp).then_inc(cmp_e, 1)
                exps(l, 1, 1, 1)
                pt_even(l, 0)
                pt_even(l, 2)
                pt_even(l, 4)
                exps(l, 2, 0, 0)
                pt_even(l, 6)
                pt_even(l, 8)
                act.wait_ge(pv_done, l * 13 + 9)
                nc.scalar.activation(o_tok[:, 1, :], bank(5), ACT.Copy).then_inc(o_ready, 1)
                exps(l, 3, 0, 1)
                pt_even(l, 10)
                pt_even(l, 12)
                for i, tt in enumerate((1, 0)):
                    act.wait_ge(oT_done, l * 2 + (i + 1))
                    nc.scalar.activation(hiB[:, 0:4, tt * P:(tt + 1) * P], bank(6 + i).rearrange("p (c t) -> p c t", c=4),
                                         ACT.Copy).then_inc(cc_hi, 1)
                hi_layer(l, 6)
                hi_layer(l, 7)
                act.wait_ge(x_ready, l * 3 + 2)
                act.wait_ge(ms_done, l * 4 + 2)
                squares(x)
                dests = [kx_T[:, 0:2, :], kx_T[:, 4:6, :], v_x[:, 0, 0:512], v_x[:, 0, 512:1024], q_x_T[:, 0:2, :], q_x_T[:, 4:6, :]]

                def kvq(i):
                    act.wait_ge(kvq_done, l * 12 + (2 * i + 1))
                    src = bank(4 + 2 * (i % 2))
                    src = src if i in (2, 3) else src.rearrange("p (c t) -> p c t", c=2)
                    nc.scalar.activation(dests[i], src, ACT.Copy).then_inc(kvq_act, 1)

                kvq(0)
                hi_layer(l, 8)
                kvq(1)
                hi_layer(l, 9)
                norm_hi(l, 2, "g_x", hiB)
                kvq(2)
                hi_layer(l, 10)
                kvq(3)
                hi_layer(l, 11)
                kvq(4)
                hi_layer(l, 12)
                kvq(5)
                hi_layer(l, 13)
                for tt in range(NT):
                    act.wait_ge(xnm_ready, l * 2 + (tt + 1))
                    for h in range(XH):
                        ins = nc.scalar.activation(p_x[:, tt, h, :], bank(2 * tt + h // 2)[:, (h % 2) * 256:(h % 2) * 256 + 256], ACT.Exp,
                                                   bias=stat[:, 16 + 4 * tt + h:17 + 4 * tt + h], scale=256 ** -0.5,
                                                   accum_out=stat[:, 32 + 4 * tt + h:33 + 4 * tt + h])
                    ins.then_inc(xexp_done, 1)
                for tt in range(NT):
                    act.wait_ge(xt2_done, l * 4 + (2 * tt + 1))
                    nc.scalar.activation(pt_x[:, :, 0:2, tt * P:(tt + 1) * P],
                                         bank(4 + 2 * tt).rearrange("p (m h t) -> p m h t", m=2, h=2), ACT.Copy).then_inc(pt2_ready, 1)
                for i in range(4):
                    act.wait_ge(ox_done, l * 4 + (i + 1))
                    nc.scalar.activation(hiA[:, 2 * i:2 * i + 2, :], bank(i).rearrange("p (c t) -> p c t", c=2), ACT.Copy).then_inc(ox_hi, 1)
                act.wait_ge(x_ready, l * 3 + 3)
                act.wait_ge(ms_done, l * 4 + 3)
                squares(x)
                norm_hi(l, 3, "g_ffn", hiB)

                with act.If(l < 1):
                    def fhi(kind, t, first=False):
                        b_l = LAYER_LOADS if kind < 2 else 0
                        if not first:
                            act.wait_ge(w_used[kind], t)
                        hi(kind, t + (b_l + 1), 2048)

                    def dense(t, first=False, last=False):
                        act.wait_ge(w_used[0], t + 1)
                        if not first:
                            act.wait_ge(f_mul, t + 0)
                        nc.scalar.activation(f_sil[:], bank(0), ACT.Silu).then_inc(f_silu, 1)
                        if not last:
                            fhi(0, t + 1)
                        fhi(2, t + 0, first)
                        act.wait_ge(f_mul, t + 1)
                        nc.scalar.activation(f_hi[:], f_act[:].rearrange("p (c t) -> p c t", c=2), ACT.Copy).then_inc(f_hi_s, 1)
                        if not last:
                            fhi(1, t + 1)

                    act.wait_ge(cross_out, 4)
                    fhi(0, 0, True)
                    fhi(1, 0, True)
                    dense(0, first=True)
                    with act.Fori(1, FF_STEPS - 1) as t:
                        dense(t)
                    dense(FF_STEPS - 1, last=True)
                    for slot in range(2):
                        act.wait_ge(w_used[slot], FF_STEPS)

            act.wait_ge(rv, 9)
            nc.scalar.activation(rt[:, 260:262], rt[:, 258:260], ACT.Exp).then_inc(r_exp, 1)

            def mhi(kind, n, first=False):
                if not first:
                    act.wait_ge(w_used[kind], n + FF_STEPS)
                hi(kind, n + (MOE_LOADS[kind] + 1))

            def item(it, first=False):
                for s in range(MOE_STEPS):
                    n = it * MOE_STEPS + s
                    begin = first and s == 0
                    if begin:
                        act.wait_ge(cross_out, 4 * DEPTH)
                    mhi(0, n, begin)
                    if s == 0:
                        act.wait_ge(gath_done, it + 1)
                        for k in range(KD):
                            ins = nc.scalar.activation(e_hi[:, k, :], bank(6 + k // 4)[:, (k % 4) * P:(k % 4) * P + P], ACT.Copy,
                                                       scale=sml("g_ffn", k, k + 1))
                        ins.then_inc(e_hi_s, 1)
                    mhi(1, n, begin)
                    if s == 1 and not first:
                        act.wait_ge(w_used[2], it * MOE_STEPS + FF_STEPS)
                        nc.scalar.activation(down_out[:, 0:512], bank(2), ACT.Copy).then_inc(md_ev, 1)
                    if not begin:
                        mhi(2, n - 1, first and s == 1)
                    act.wait_ge(w_used[0], n + (FF_STEPS + 1))
                    if not begin:
                        act.wait_ge(m_mul, n + 0)
                    nc.scalar.activation(hid_tok[:, 0, :], bank(0), ACT.Silu).then_inc(m_silu, 1)
                    if not begin:
                        act.wait_ge(mt_done, n + 0)
                        nc.scalar.activation(a_hi[:], bank(4), ACT.Copy).then_inc(ma_hi, 1)
                    if s == 5:
                        act.wait_ge(ohT_done, it + 1)
                        nc.scalar.activation(onehot_gT[:], bank(5)[:, 0:SEQ], ACT.Copy).then_inc(ohT_ready, 1)

            item(0, first=True)
            act.wait_ge(items_ready, 1)
            n_items = act.value_load(items_i[0:1, NCOL:NCOL + 1], min_val=E, max_val=2 * E)
            with act.Fori(1, n_items) as it:
                item(it)
            mhi(2, n_items * MOE_STEPS - 1)
            act.wait_ge(mt_done, n_items * MOE_STEPS)
            nc.scalar.activation(a_hi[:], bank(4), ACT.Copy).then_inc(ma_hi, 1)
            act.wait_ge(w_used[2], n_items * MOE_STEPS + FF_STEPS)
            nc.scalar.activation(down_out[:, 0:512], bank(2), ACT.Copy).then_inc(md_ev, 1)
            act.wait_ge(x_ready, 3 * DEPTH + 1)
            squares(x)

        @block.tensor
        def _(pe):
            mm = nc.tensor.matmul

            def product(out, ah, al, bh, bl, start, stop):
                mm(out, ah, bh, start=start, stop=False)
                mm(out, ah, bl, start=False, stop=False)
                return mm(out, al, bh, start=False, stop=stop)

            def norm_T(l, j):
                pe.wait_ge(xs_ready, l * 4 + (j + 1))
                for i in range(4):
                    for k in (2 * i, 2 * i + 1):
                        for t in range(NT):
                            ins = nc.tensor.transpose(bank(i)[:, (k % 2) * 256 + t * P:(k % 2) * 256 + (t + 1) * P],
                                                      xs[:, t, k * P:(k + 1) * P], ident)
                    ins.then_inc(xT_done, 1)

            def weights(slot, n=512):
                w = slice(0, KD * n)
                return (whi[slot][:, w].rearrange("p (k n) -> p k n", k=KD), wlo[slot][:, w].rearrange("p (k n) -> p k n", k=KD))

            def head(h):
                return slice((h // GRP) * HD, (h // GRP) * HD + HD), h % GRP

            def scores(l, u, br, tt):
                nk, b0 = P * (tt + 1), (2 if u == 3 else 0)
                nb = HEADS * nk // 512
                mask = causal_bf[:, 256 - nk:256]
                for b in range(nb):
                    hb = 512 // nk
                    rows = mask.unsqueeze(1).to_broadcast([P, hb, nk])
                    mm(bank(b0 + b).rearrange("p (h n) -> p h n", h=hb), ident_bf[:], rows, start=True, stop=False,
                       skip_group_check=True)
                for h in range(HEADS):
                    rows, c = head(h)
                    b, o_ = divmod(h * nk, 512)
                    ins = mm(bank(b0 + b)[:, o_:o_ + nk], q_rot_T[rows, c, tt * P:(tt + 1) * P], k_T[rows, br, 0:nk],
                             start=False, stop=True, skip_group_check=True)
                ins.then_inc(s_done, 1)

            units = [(0, 1, 0), (1, 1, 1), (0, 0, 0), (1, 0, 1)]
            groups = []
            for u, (br, tt, slot) in enumerate(units):
                nk = tt + 1
                tiles = [(h, kc) for h in range(HEADS) for kc in range(nk)]
                for i in range(0, len(tiles), 4):
                    groups.append((u, tiles[i:i + 4]))
                if u == 0:
                    groups.append(None)

            def transpose_group(l, i):
                g = groups[i]
                if i >= 2:
                    pe.wait_ge(pt_act if i % 2 == 0 else pt_dve, l * (7 if i % 2 == 0 else 6) + i // 2)
                if g is None:
                    pe.wait_ge(pc_ready, l + 1)
                    for q in range(4):
                        ins = nc.tensor.transpose(bank(6 + i % 2)[:, q * P:(q + 1) * P],
                                                  p_cmp[:, 4 * q:4 * q + 4, :].rearrange("p c s -> p (c s)"), ident)
                else:
                    u, tiles = g
                    br, tt, slot = units[u]
                    nk = P * (tt + 1)
                    pe.wait_ge(p_ready, l * 4 + (u + 1))
                    for q, (h, kc) in enumerate(tiles):
                        a = h * nk + kc * P
                        ins = nc.tensor.transpose(bank(6 + i % 2)[:, q * P:(q + 1) * P], probs[slot][:, a:a + P], ident)
                ins.then_inc(t_done, 1)

            def pv_group(l, i):
                g = groups[i]
                pe.wait_ge(pt_act if i % 2 == 0 else pt_dve, l * (7 if i % 2 == 0 else 6) + (i // 2 + 1))
                src = pt[i % 2]
                if g is None:
                    for q in range(4):
                        gg, tt = divmod(q, 2)
                        ins = mm(bank(4 + tt)[:, gg * 256:(gg + 1) * 256], src[:, q * P:(q + 1) * P], v_bd[:, gg, :],
                                 start=(tt == 0 and gg == 0), stop=True, skip_group_check=True)
                else:
                    u, tiles = g
                    br, tt, slot = units[u]
                    for q, (h, kc) in enumerate(tiles):
                        v = z[:, kc, (Z_VSLC if br == 0 else Z_VWIN) + (h // GRP) * HD:(Z_VSLC if br == 0 else Z_VWIN) + (h // GRP) * HD + HD]
                        ins = mm(bank(4 + tt)[:, h * HD:(h + 1) * HD], src[:, q * P:(q + 1) * P], v,
                                 start=(i == 0 and q == 0), stop=True, skip_group_check=True)
                ins.then_inc(pv_done, 1)
                return ins

            pe.wait_ge(const_in, 32)
            pe.wait_ge(consts_ready, 4)
            with pe.Fori(0, DEPTH) as l:
                norm_T(l, 0)
                for c in range(4):
                    pe.wait_ge(w_lo[c % 2], l * PER_LAYER_SPLITS + (c // 2 + 1))
                    wh, wl = weights(c % 2, ZW)
                    if c >= 2:
                        pe.wait_ge(z_act, l * 4 + (c - 1))
                        pe.wait_ge(z_dve, l * 4 + (c - 1))
                    for t in range(NT):
                        for k in range(KD):
                            if c == 0 and t == 0 and k % 2 == 0:
                                pe.wait_ge(n_lo, l * 16 + (k // 2 + 1))
                            tok = slice(t * P, (t + 1) * P)
                            ins = product(bank(4 + 2 * (c % 2) + t)[:, 0:ZW], hiA[:, k, tok], loA[:, k, tok], wh[:, k, :], wl[:, k, :],
                                          k == 0, k == KD - 1)
                        ins.then_inc(z_done, 1)
                norm_T(l, 1)
                pe.wait_ge(rope_done, l + 1)
                pe.wait_ge(z_act, l * 4 + 4)
                pe.wait_ge(z_dve, l * 4 + 4)
                for b in range(3):
                    for c in (2 * b, 2 * b + 1):
                        for t in range(NT):
                            ins = nc.tensor.transpose(bank(4 + b)[:, (c % 2) * 256 + t * P:(c % 2) * 256 + (t + 1) * P],
                                                      qk_rot[:, t, c * P:(c + 1) * P], ident)
                    ins.then_inc(tq_done, 1)
                for kv in range(2):
                    for g in range(2):
                        for t in range(NT):
                            for par in range(2):
                                col = kv * 256 + g * 128 + t * 64
                                ins = mm(bank(7)[par * 64:par * 64 + 64, col:col + 64],
                                         z[:, t, Z_KCMP + kv * 128 + g * 64:Z_KCMP + kv * 128 + g * 64 + 64],
                                         ident[:, par::2], start=True, stop=True)
                ins.then_inc(xt_done, 1)
                pe.wait_ge(n_lo, l * 16 + 8)
                pe.wait_ge(n_hi, l * 16 + 8)
                for b in range(2):
                    for c in (2 * b, 2 * b + 1):
                        for t in range(NT):
                            ins = nc.tensor.transpose(bank(b)[:, (c % 2) * 256 + t * P:(c % 2) * 256 + (t + 1) * P],
                                                      z[:, t, c * P:(c + 1) * P], ident)
                    ins.then_inc(tr_done, 1)
                for g in range(4):
                    out = bank(2 + g // 2)[:, (g % 2) * 256:(g % 2) * 256 + 256]
                    u0 = Z_U + g * P
                    mm(out, z[:, 0, u0:u0 + P], cst("band", g * 384, g * 384 + 256), start=True, stop=False, skip_group_check=True)
                    ins = mm(out[:, P:256], z[:, 1, u0:u0 + P], cst("band", g * 384 + 256, (g + 1) * 384), start=False, stop=True,
                             skip_group_check=True)
                    if g % 2:
                        ins.then_inc(pd_done, 1)
                pe.wait_ge(q_rot_ready, l * 3 + 3)
                pe.wait_ge(q_raw_ready, l * 2 + 2)
                pe.wait_ge(d_ready, l * 2 + 2)
                scores(l, 0, 0, 1)
                for kv in range(2):
                    pe.wait_ge(blk_ready, l * 2 + (kv + 1))
                    pe.wait_ge(w_in_ring[kv], (l * PER_LAYER_LOADS + 3) * 16)
                    w1 = stage[kv][:].rearrange("p (j n) -> p j n", j=CMP_J)
                    for hc in range(2):
                        g = kv * 2 + hc
                        for j in range(CMP_J):
                            ins = mm(bank(6)[:, g * 32:g * 32 + 2 * N_CMP], w1[:, j, hc * P:(hc + 1) * P], blk_T[:, kv, j, :],
                                     start=(j == 0), stop=(j == CMP_J - 1))
                    ins.then_inc(hid_done, 1)
                for g in range(4):
                    ins = mm(bank(4 + g // 2)[:, (g % 2) * 256:(g % 2) * 256 + 256], sml("w_pool", g * P, (g + 1) * P), d_T[:, g, :],
                             start=True, stop=True)
                    if g % 2:
                        ins.then_inc(y_done, 1)
                pe.wait_ge(gelu_done, l * 2 + 2)
                for g in range(2):
                    for hc in range(2):
                        mm(bank(7)[g * HD:(g + 1) * HD, 0:N_CMP], sml("w2k", hc * HD, (hc + 1) * HD),
                           hid[:, 0, hc, g * N_CMP:(g + 1) * N_CMP], start=(hc == 0), stop=(hc == 1))
                for g in range(2):
                    for hc in range(2):
                        ins = mm(bank(7)[0:N_CMP, 64 + g * HD:64 + (g + 1) * HD], hid[:, 1, hc, g * N_CMP:(g + 1) * N_CMP],
                                 sml("w2v", hc * HD, (hc + 1) * HD), start=(hc == 0), stop=(hc == 1))
                ins.then_inc(kcvc_done, 1)
                pe.wait_ge(kcvc_ready, l + 1)
                for h in range(HEADS):
                    rows, c = head(h)
                    for t in range(NT):
                        col = (t * GRP + c) * 16
                        ins = mm(bank(6 + h // GRP)[:, col:col + N_CMP], q_raw_T[rows, c, t * P:(t + 1) * P], k_cmp_T[rows, 0:N_CMP],
                                 start=True, stop=True)
                ins.then_inc(cs_done, 1)
                pe.wait_ge(exps_done, l * 4 + 1)
                scores(l, 1, 1, 1)
                pe.wait_ge(y_hi, l * 2 + 2)
                pe.wait_ge(y_lo, l * 2 + 2)
                pe.wait_ge(cmp_v, l * 8 + 2)
                for i in range(len(groups) + 1):
                    if i < len(groups):
                        if i == 5:
                            pe.wait_ge(exps_done, l * 4 + 2)
                            scores(l, 2, 0, 0)
                            scores(l, 3, 1, 0)
                        transpose_group(l, i)
                    if i >= 1:
                        pv_group(l, i - 1)
                for i, tt in enumerate((1, 0)):
                    pe.wait_ge(o_ready, l * 2 + (i + 1))
                    for c in range(4):
                        ins = nc.tensor.transpose(bank(6 + i)[:, c * P:(c + 1) * P], o_tok[:, tt, c * P:(c + 1) * P], ident)
                    ins.then_inc(oT_done, 1)
                pe.wait_ge(cc_lo, l * 2 + 2)
                for hf in range(2):
                    s = 4 + hf
                    pe.wait_ge(w_lo[hf], l * PER_LAYER_SPLITS + (s // 2 + 1))
                    wh, wl = weights(hf)
                    for t in range(NT):
                        tok = slice(t * P, (t + 1) * P)
                        for k in range(KD):
                            ins = product(bank(2 * hf + t), hiB[:, k, tok], loB[:, k, tok], wh[:, k, :], wl[:, k, :], k == 0, k == KD - 1)
                        ins.then_inc(mix_out, 1)

                def by_feature(i, s, ah, al):
                    pe.wait_ge(w_lo[s % 2], l * PER_LAYER_SPLITS + (s // 2 + 1))
                    wh, wl = weights(s % 2)
                    if i >= 2:
                        pe.wait_ge(kvq_act, l * 6 + (i - 1))
                        pe.wait_ge(kvq_dve, l * 6 + (i - 1))
                    for n in range(4):
                        out = bank(4 + 2 * (i % 2) + n // 2)[:, (n % 2) * 256:(n % 2) * 256 + 256]
                        for k in range(KD):
                            cols = slice(n * P, (n + 1) * P)
                            ins = product(out, wh[:, k, cols], wl[:, k, cols], ah[:, k, :], al[:, k, :], k == 0, k == KD - 1)
                        if n % 2:
                            ins.then_inc(kvq_done, 1)

                by_feature(0, 6, hiA, loA)
                by_feature(1, 7, hiA, loA)
                norm_T(l, 2)
                for hf in range(2):
                    s, i = 8 + hf, 2 + hf
                    pe.wait_ge(w_lo[hf], l * PER_LAYER_SPLITS + (s // 2 + 1))
                    wh, wl = weights(hf)
                    pe.wait_ge(kvq_act, l * 6 + (i - 1))
                    pe.wait_ge(kvq_dve, l * 6 + (i - 1))
                    for t in range(NT):
                        tok = slice(t * P, (t + 1) * P)
                        for k in range(KD):
                            ins = product(bank(4 + 2 * hf + t), hiA[:, k, tok], loA[:, k, tok], wh[:, k, :], wl[:, k, :], k == 0, k == KD - 1)
                        ins.then_inc(kvq_done, 1)
                pe.wait_ge(n_lo, l * 16 + 12)
                by_feature(4, 10, hiB, loB)
                by_feature(5, 11, hiB, loB)
                pe.wait_ge(kvq_act, l * 6 + 6)
                pe.wait_ge(kvq_dve, l * 6 + 6)
                for t in range(NT):
                    for h in range(XH):
                        out = bank(2 * t + h // 2)[:, (h % 2) * 256:(h % 2) * 256 + 256]
                        for dc in range(2):
                            ins = mm(out, q_x_T[:, 2 * h + dc, t * P:(t + 1) * P], kx_T[:, 2 * h + dc, :], start=(dc == 0), stop=(dc == 1))
                    ins.then_inc(xs_done, 1)
                for t in range(NT):
                    pe.wait_ge(xp_ready, l * 2 + (t + 1))
                    for hp in range(2):
                        for m in range(2):
                            for h2 in range(2):
                                col = (m * 2 + h2) * P
                                ins = nc.tensor.transpose(bank(4 + 2 * t + hp)[:, col:col + P], p_x[:, t, 2 * hp + h2, m * P:(m + 1) * P], ident)
                        ins.then_inc(xt2_done, 1)
                pe.wait_ge(pt2_ready, l * 4 + 4)
                for h in range(XH):
                    for dc in range(2):
                        for m in range(2):
                            ins = mm(bank(h)[:, dc * 256:(dc + 1) * 256], v_x[:, m, h * 256 + dc * P:h * 256 + (dc + 1) * P], pt_x[:, m, h, :],
                                     start=(m == 0), stop=(m == 1))
                    ins.then_inc(ox_done, 1)
                for hf in range(2):
                    s = 12 + hf
                    pe.wait_ge(w_lo[hf], l * PER_LAYER_SPLITS + (s // 2 + 1))
                    wh, wl = weights(hf)
                    for t in range(NT):
                        tok = slice(t * P, (t + 1) * P)
                        for k in range(KD):
                            if hf == 0 and t == 0 and k % 2 == 0:
                                pe.wait_ge(ox_lo, l * 4 + (k // 2 + 1))
                            ins = product(bank(4 + 2 * hf + t), hiA[:, k, tok], loA[:, k, tok], wh[:, k, :], wl[:, k, :], k == 0, k == KD - 1)
                        ins.then_inc(cross_out, 1)
                norm_T(l, 3)
                pe.wait_ge(n_lo, l * 16 + 16)

                with pe.If(l < 1):
                    def wf(kind):
                        k = KD if kind < 2 else 2
                        return (whi[kind][:, 0:2048].rearrange("p (k n) -> p k n", k=k), wlo[kind][:, 0:2048].rearrange("p (k n) -> p k n", k=k))

                    def up(kind, t, first):
                        pe.wait_ge(w_lo[kind], t + (LAYER_SPLITS + 1))
                        wh, wl = wf(kind)
                        if not first:
                            pe.wait_ge(f_silu if kind == 0 else f_mul, t + 0)
                        for n in range(2):
                            for k in range(KD):
                                cols = slice(n * P, (n + 1) * P)
                                ins = product(bank(kind)[:, n * 256:(n + 1) * 256], wh[:, k, cols], wl[:, k, cols], hiB[:, k, :], loB[:, k, :],
                                              k == 0, k == KD - 1)
                        ins.then_inc(w_used[kind], 1)

                    def down(t, first=False, last=False):
                        pe.wait_ge(w_lo[2], t + 1)
                        pe.wait_ge(f_lo_s, t + 1)
                        wh, wl = wf(2)
                        for tt in range(NT):
                            tok = slice(tt * P, (tt + 1) * P)
                            for hf in range(2):
                                cols = slice(hf * 512, (hf + 1) * 512)
                                for c in range(2):
                                    ins = product(bank(4 + 2 * tt + hf), f_hi[:, c, tok], f_lo[:, c, tok], wh[:, c, cols], wl[:, c, cols],
                                                  first and c == 0, last and c == 1)
                        ins.then_inc(w_used[2], 1)

                    up(0, 0, True)
                    up(1, 0, True)
                    up(0, 1, False)
                    down(0, first=True)
                    up(1, 1, False)
                    with pe.Fori(2, FF_STEPS) as t:
                        up(0, t, False)
                        down(t - 1)
                        up(1, t, False)
                    down(FF_STEPS - 1, last=True)

            for t in range(NT):
                tok = slice(t * P, (t + 1) * P)
                for k in range(KD):
                    mm(bank(0)[:, t * E:(t + 1) * E], f32(hiB[:, k, tok]), router[:, k, :], start=(k == 0), stop=False)
                    ins = mm(bank(0)[:, t * E:(t + 1) * E], f32(loB[:, k, tok]), router[:, k, :], start=False, stop=(k == KD - 1))
            ins.then_inc(lg_done, 1)
            pe.wait_ge(rv, 7)
            member = rt[:, 240:256]
            below, one = cst("below"), ones[:]
            mm(bank(1)[:, 0:E], below, member[:, 0:E], start=True, stop=True)
            mm(bank(1)[:, E:2 * E], one, member[:, 0:E], start=True, stop=False)
            mm(bank(1)[:, E:2 * E], below, member[:, E:2 * E], start=False, stop=True)
            mm(bank(1)[:, 2 * E:3 * E], one, member[:, 0:E], start=True, stop=False)
            mm(bank(1)[:, 2 * E:3 * E], one, member[:, E:2 * E], start=False, stop=True).then_inc(pos_done, 1)

            def gather(it):
                pe.wait_ge(oh_ready, it + 1)
                for k in range(KD):
                    for t in range(NT):
                        ins = mm(bank(6 + k // 4)[:, (k % 4) * P:(k % 4) * P + CAP], xs[:, t, k * P:(k + 1) * P], onehot[:, t, :],
                                 start=(t == 0), stop=(t == NT - 1))
                ins.then_inc(gath_done, 1)

            def turn(n):
                pe.wait_ge(m_mul, n)
                for c in range(4):
                    ins = nc.tensor.transpose(bank(4)[:, c * P:(c + 1) * P], hid_tok[:, 1, c * P:(c + 1) * P], ident)
                ins.then_inc(mt_done, 1)

            def down_e(n, start, stop):
                pe.wait_ge(w_lo[2], n + MOE_SPLITS[2])
                pe.wait_ge(ma_lo, n)
                wh = whi[2][:].rearrange("p (c n) -> p c n", c=4)
                wl = wlo[2][:].rearrange("p (c n) -> p c n", c=4)
                for hf in range(2):
                    cols = slice(hf * 512, (hf + 1) * 512)
                    for c in range(4):
                        ins = product(bank(2 + hf), a_hi[:, c * P:(c + 1) * P], a_lo[:, c * P:(c + 1) * P], wh[:, c, cols], wl[:, c, cols],
                                      start and c == 0, stop and c == 3)
                ins.then_inc(w_used[2], 1)

            def scatter(it, j):
                t, hf = divmod(j, 2)
                if j == 0:
                    pe.wait_ge(md_ev, it * 2)
                    pe.wait_ge(ohT_ready, it)
                if j:
                    pe.wait_ge(sc_add, it * 4 + j)
                mm(bank(5), onehot_gT[:, t * P:(t + 1) * P], down_out[:, hf * 512:(hf + 1) * 512], start=True, stop=True).then_inc(sc_done, 1)

            def item(it, first=False):
                for s in range(MOE_STEPS):
                    n = it * MOE_STEPS + s
                    begin = first and s == 0
                    for kind in range(2):
                        pe.wait_ge(w_lo[kind], n + (MOE_SPLITS[kind] + 1))
                        wh, wl = weights(kind)
                        if kind == 0:
                            if s == 0:
                                pe.wait_ge(e_lo_s, it + 1)
                            if not begin:
                                pe.wait_ge(m_silu, n)
                        for k in range(KD):
                            ins = product(bank(kind), e_hi[:, k, :], e_lo[:, k, :], wh[:, k, :], wl[:, k, :], k == 0, k == KD - 1)
                        ins.then_inc(w_used[kind], 1)
                        if kind == 0 and not begin:
                            turn(n)
                    if s == MOE_STEPS - 1:
                        gather(it + 1)
                    if not begin:
                        if s == 1 and not first:
                            pe.wait_ge(md_ev, it * 2)
                        down_e(n, s == 1, s == 0)
                    if 1 <= s <= 4 and not first:
                        scatter(it, s - 1)
                    if s == 5:
                        pe.wait_ge(oh_g_ready, it + 1)
                        if not first:
                            pe.wait_ge(sc_add, it * 4 + 4)
                        for t in range(NT):
                            ins = nc.tensor.transpose(bank(5)[:, t * P:(t + 1) * P], onehot_g[:, t, :], ident)
                        ins.then_inc(ohT_done, 1)

            gather(0)
            item(0, first=True)
            pe.wait_ge(items_ready, 1)
            n_items = pe.value_load(items_i[0:1, NCOL:NCOL + 1], min_val=E, max_val=2 * E)
            with pe.Fori(1, n_items) as it:
                item(it)
            turn(n_items * MOE_STEPS)
            down_e(n_items * MOE_STEPS, False, True)
            for j in range(4):
                scatter(n_items, j)

        @block.vector
        def _(dve):
            V = nc.vector

            def lo(slot, fill, n=4096):
                dve.wait_ge(w_hi[slot], fill)
                V.tensor_tensor(wlo[slot][:, 0:n], stage[slot][:, 0:n], f32(whi[slot][:, 0:n]), ALU.subtract).then_inc(w_lo[slot], 1)

            def lo_layer(l, s):
                lo(s % 2, l * PER_LAYER_SPLITS + (s // 2 + 1), KD * ZW if s < 4 else 4096)

            def norm_scale(src, n):
                dve.wait_ge(ssq_done, n)
                V.tensor_scalar(stat[:, 4:6], stat[:, 0:2], 1.0 / D, EPS, ALU.mult, ALU.add).then_inc(ms_done, 1)
                dve.wait_ge(rstd_done, n)
                for t in range(NT):
                    ins = V.tensor_scalar(xs[:, t, :], src[:, t, :], stat[:, 6 + t:7 + t], None, ALU.mult)
                ins.then_inc(xs_ready, 1)

            def norm_lo(l, j, gain, hi_, lo_):
                for i in range(4):
                    dve.wait_ge(n_hi, l * 16 + (4 * j + i + 1))
                    for k in (2 * i, 2 * i + 1):
                        ins = V.scalar_tensor_tensor(out=lo_[:, k, :], in0=bank(i)[:, (k % 2) * 256:(k % 2) * 256 + 256],
                                                     scalar=sml(gain, k, k + 1), in1=f32(hi_[:, k, :]), op0=ALU.mult, op1=ALU.subtract)
                    ins.then_inc(n_lo, 1)

            def unit_max(l, u, tt, slot):
                nk = P * (tt + 1)
                b0 = 2 if u == 3 else 0
                dve.wait_ge(s_done, l * 4 + (u + 1))
                sc = PS[:, b0:b0 + HEADS * nk // 512, :].rearrange("p b (h n) -> p (b h) n", n=nk)
                V.tensor_reduce(stat[:, 8:16], sc, AX, ALU.max).then_inc(max_done, 1)
                dve.wait_ge(max_done, l * 4 + (u + 1))
                V.tensor_scalar(stat[:, 16 + 8 * slot:24 + 8 * slot], stat[:, 8:16], -(HD ** -0.5), None, ALU.mult).then_inc(nm_ready, 1)

            def unit_scale(l, u, br, tt, slot):
                nk = P * (tt + 1)
                dve.wait_ge(exps_done, l * 4 + (u + 1))
                r = stat[:, 48:56]
                V.reciprocal(r, stat[:, 32 + 8 * slot:40 + 8 * slot]).then_inc(r_done, 1)
                dve.wait_ge(r_done, l * 8 + (2 * u + 1))
                dve.wait_ge(gate_v, l * 3 + 2)
                V.tensor_tensor(r, r, gates[:, tt, 1 + br::3], ALU.mult).then_inc(r_done, 1)
                dve.wait_ge(r_done, l * 8 + (2 * u + 2))
                pr = probs[slot][:, 0:HEADS * nk].rearrange("p (h n) -> p h n", h=HEADS)
                V.tensor_tensor(pr, pr, r.unsqueeze(2).to_broadcast([P, HEADS, nk]), ALU.mult).then_inc(p_ready, 1)

            def pt_odd(l, i):
                dve.wait_ge(t_done, l * 13 + (i + 1))
                if i >= 2:
                    dve.wait_ge(pv_done, l * 13 + (i - 1))
                V.tensor_copy(pt[1][:], bank(7)).then_inc(pt_dve, 1)

            V.memset(stat[:, 57:58], 0.0).then_inc(sc_add, 4)
            V.memset(stat[:, 58:59], 0.0).then_inc(sc_done, 4)
            V.memset(stat[:, 56:57], 0.0).then_inc(x_ready, 1)
            dve.wait_ge(const_in, 32)
            dve.wait_ge(mask_in, 16)
            V.tensor_copy(ident_bf[:], ident).then_inc(consts_ready, 1)
            V.tensor_copy(causal_bf[:], cmask_f[:]).then_inc(consts_ready, 1)
            dve.wait_ge(consts_ready, 4)
            dve.wait_ge(x_in, 16)
            with dve.Fori(0, DEPTH) as l:
                norm_scale(x, l * 4 + 1)
                lo_layer(l, 0)
                dve.wait_ge(small_in, l * 16 + 16)
                norm_lo(l, 0, "g_mix", hiA, loA)
                lo_layer(l, 1)
                for c in range(4):
                    dve.wait_ge(z_done, l * 8 + (2 * c + 2))
                    V.tensor_copy(z[:, 1, c * ZW:(c + 1) * ZW], bank(5 + 2 * (c % 2))[:, 0:ZW]).then_inc(z_dve, 1)
                    if c == 1:
                        dve.wait_ge(z_act, l * 4 + 2)
                        dve.wait_ge(z_dve, l * 4 + 2)
                        rot_in = z[:, :, 0:768].rearrange("p t (h d) -> p t h d", d=HD)[:, :, :, 0:ROPE]
                        for n, (dst, tab) in enumerate(((rope_c, "cos"), (rope_s, "sin"))):
                            t_ = cst(tab).rearrange("p (t r) -> p t r", t=NT).unsqueeze(2).to_broadcast([P, NT, 12, ROPE])
                            for t in range(NT):
                                ins = V.tensor_tensor(dst[:, t], rot_in[:, t], t_[:, t], ALU.mult)
                        ins.then_inc(rope_part, 1)
                    if c < 2:
                        lo_layer(l, c + 2)
                    if c == 1:
                        dve.wait_ge(rope_part, l + 1)
                        dve.wait_ge(qk_copied, l + 1)
                        q4 = qk_rot[:].rearrange("p t (h d) -> p t h d", d=HD)
                        V.tensor_tensor(q4[:, :, :, 0:8], rope_c[:, :, :, 0:8], rope_s[:, :, :, 8:16], ALU.subtract)
                        V.tensor_tensor(q4[:, :, :, 8:16], rope_c[:, :, :, 8:16], rope_s[:, :, :, 0:8], ALU.add).then_inc(rope_done, 1)
                norm_scale(xs, l * 4 + 2)
                norm_lo(l, 1, "g_mem", hiA, loA)
                dve.wait_ge(gate_e, l + 1)
                V.tensor_scalar(gates[:], gates[:], 1.0, None, ALU.add).then_inc(gate_v, 1)
                dve.wait_ge(gate_v, l * 3 + 1)
                V.reciprocal(gates[:], gates[:]).then_inc(gate_v, 1)
                dve.wait_ge(tq_done, l * 3 + 2)
                V.tensor_copy(q_rot_T[:, 2:4, :], bank(5).rearrange("p (c t) -> p c t", c=2)).then_inc(q_rot_ready, 1)
                dve.wait_ge(xt_done, l + 1)
                for kv in range(2):
                    for g in range(2):
                        src = bank(7)[:, kv * 256 + g * 128:kv * 256 + (g + 1) * 128]
                        pe_ = sml("pe", kv * CMP_J, (kv + 1) * CMP_J)
                        for half in range(2):
                            s_ = src[:, half * 8:half * 8 + 8 * N_CMP].rearrange("p (c j) -> p j c", j=8)
                            ins = V.tensor_tensor(blk_T[:, kv, half * 8:half * 8 + 8, g * N_CMP:(g + 1) * N_CMP], s_,
                                                  pe_[:, half * 8:half * 8 + 8].unsqueeze(2).to_broadcast([P, 8, N_CMP]), ALU.add)
                    ins.then_inc(blk_ready, 1)
                dve.wait_ge(tr_done, l * 2 + 2)
                V.tensor_copy(q_raw_T[:, 2:4, :], bank(1).rearrange("p (c t) -> p c t", c=2)).then_inc(q_raw_ready, 1)
                dve.wait_ge(pd_done, l * 2 + 2)
                V.tensor_copy(d_T[:, 2:4, :], bank(3).rearrange("p (c t) -> p c t", c=2)).then_inc(d_ready, 1)
                lo_layer(l, 4)
                lo_layer(l, 5)
                unit_max(l, 0, 1, 0)
                for i in range(2):
                    dve.wait_ge(y_hi, l * 2 + (i + 1))
                    for g in (2 * i, 2 * i + 1):
                        ins = V.scalar_tensor_tensor(out=loB[:, 4 + g, :], in0=bank(4 + i)[:, (g % 2) * 256:(g % 2) * 256 + 256],
                                                     scalar=sml("pool_scale", g, g + 1), in1=f32(hiB[:, 4 + g, :]), op0=ALU.mult, op1=ALU.subtract)
                    ins.then_inc(y_lo, 1)
                dve.wait_ge(kcvc_done, l + 1)
                V.tensor_copy(k_cmp_T[:, 0:N_CMP], bank(7)[:, 0:N_CMP])
                for i in range(4):
                    ins = V.tensor_copy(v_bd[32 * i:32 * i + N_CMP, :, i * HD:(i + 1) * HD],
                                        bank(7)[0:N_CMP, 64:192].rearrange("p (g d) -> p g d", g=2))
                ins.then_inc(kcvc_ready, 1)
                unit_scale(l, 0, 0, 1, 0)
                lc = l_cmp[:, :, 0:N_CMP]
                dve.wait_ge(cs_done, l + 1)
                cm = cst("cmp_mask").rearrange("p (r c) -> p r c", c=16)[:, :, 0:N_CMP]
                for g in range(2):
                    src = bank(6 + g)[:, 0:128].rearrange("p (r c) -> p r c", c=16)[:, :, 0:N_CMP]
                    V.scalar_tensor_tensor(out=l_cmp[:, 8 * g:8 * g + 8, 0:N_CMP], in0=src, scalar=HD ** -0.5, in1=cm,
                                           op0=ALU.mult, op1=ALU.add).then_inc(cmp_v, 1)
                dve.wait_ge(cmp_v, l * 8 + 2)
                cmax = stat[:, 64:80]
                V.tensor_reduce(cmax, lc, AX, ALU.max).then_inc(cmp_v, 1)
                dve.wait_ge(cmp_v, l * 8 + 3)
                V.tensor_scalar(cmax, cmax, 1e-10 * NEG, None, ALU.max).then_inc(cmp_v, 1)
                dve.wait_ge(cmp_v, l * 8 + 4)
                V.tensor_tensor(lc, lc, cmax.unsqueeze(2).to_broadcast([P, 16, N_CMP]), ALU.subtract)
                V.memset(l_cmp[:, :, N_CMP:16], NEG).then_inc(cmp_v, 1)
                unit_max(l, 1, 1, 1)
                pt_odd(l, 1)
                dve.wait_ge(cmp_e, l + 1)
                V.tensor_reduce(cmax, lc, AX, ALU.add).then_inc(cmp_v, 1)
                dve.wait_ge(cmp_v, l * 8 + 6)
                V.tensor_scalar(cmax, cmax, 1.1754943508222875e-38, None, ALU.max).then_inc(cmp_v, 1)
                dve.wait_ge(cmp_v, l * 8 + 7)
                V.reciprocal(cmax, cmax).then_inc(cmp_v, 1)
                dve.wait_ge(cmp_v, l * 8 + 8)
                cr = cmax.rearrange("p (g t c) -> p g t c", g=2, t=NT)
                for g in range(2):
                    ins = V.tensor_tensor(cr[:, g], cr[:, g], gates[:, :, 12 * g:12 * g + 12:3], ALU.mult)
                ins.then_inc(gate_v, 1)
                dve.wait_ge(gate_v, l * 3 + 3)
                dve.wait_ge(p_cmp_zero, l + 1)
                V.tensor_tensor(p_cmp[:, :, 0:N_CMP], lc, cmax.unsqueeze(2).to_broadcast([P, 16, N_CMP]), ALU.mult).then_inc(pc_ready, 1)
                pt_odd(l, 3)
                unit_scale(l, 1, 1, 1, 1)
                unit_max(l, 2, 0, 0)
                pt_odd(l, 5)
                unit_scale(l, 2, 0, 0, 0)
                pt_odd(l, 7)
                unit_max(l, 3, 0, 1)
                pt_odd(l, 9)
                unit_scale(l, 3, 1, 0, 1)
                pt_odd(l, 11)
                dve.wait_ge(pv_done, l * 13 + 13)
                V.tensor_copy(o_tok[:, 0, :], bank(4)).then_inc(o_ready, 1)
                for i, tt in enumerate((1, 0)):
                    dve.wait_ge(cc_hi, l * 2 + (i + 1))
                    tok = slice(tt * P, (tt + 1) * P)
                    V.tensor_tensor(loB[:, 0:4, tok], bank(6 + i).rearrange("p (c t) -> p c t", c=4), f32(hiB[:, 0:4, tok]),
                                    ALU.subtract).then_inc(cc_lo, 1)

                def add(src_bank, t, hf):
                    xv = x[:, t, hf * 512:(hf + 1) * 512]
                    return V.tensor_tensor(xv, xv, bank(src_bank), ALU.add)

                lo_layer(l, 6)
                for hf in range(2):
                    for t in range(NT):
                        dve.wait_ge(mix_out, l * 4 + (2 * hf + t + 1))
                        ins = add(2 * hf + t, t, hf)
                    if hf == 0:
                        lo_layer(l, 7)
                ins.then_inc(x_ready, 1)
                norm_scale(x, l * 4 + 3)
                dests = [kx_T[:, 2:4, :], kx_T[:, 6:8, :], v_x[:, 1, 0:512], v_x[:, 1, 512:1024], q_x_T[:, 2:4, :], q_x_T[:, 6:8, :]]

                def kvq(i):
                    dve.wait_ge(kvq_done, l * 12 + (2 * i + 2))
                    src = bank(5 + 2 * (i % 2))
                    src = src if i in (2, 3) else src.rearrange("p (c t) -> p c t", c=2)
                    V.tensor_copy(dests[i], src).then_inc(kvq_dve, 1)

                kvq(0)
                lo_layer(l, 8)
                kvq(1)
                lo_layer(l, 9)
                norm_lo(l, 2, "g_x", hiB, loB)
                kvq(2)
                lo_layer(l, 10)
                kvq(3)
                lo_layer(l, 11)
                kvq(4)
                lo_layer(l, 12)
                kvq(5)
                lo_layer(l, 13)
                for t in range(NT):
                    dve.wait_ge(xs_done, l * 2 + (t + 1))
                    sc = PS[:, 2 * t:2 * t + 2, :].rearrange("p b (h n) -> p (b h) n", n=SEQ)
                    V.tensor_reduce(stat[:, 8 + 4 * t:12 + 4 * t], sc, AX, ALU.max).then_inc(xmax_done, 1)
                    dve.wait_ge(xmax_done, l * 2 + (t + 1))
                    V.tensor_scalar(stat[:, 16 + 4 * t:20 + 4 * t], stat[:, 8 + 4 * t:12 + 4 * t], -(256 ** -0.5), None,
                                    ALU.mult).then_inc(xnm_ready, 1)
                for t in range(NT):
                    dve.wait_ge(xexp_done, l * 2 + (t + 1))
                    r = stat[:, 48 + 4 * t:52 + 4 * t]
                    V.reciprocal(r, stat[:, 32 + 4 * t:36 + 4 * t]).then_inc(xr_done, 1)
                    dve.wait_ge(xr_done, l * 2 + (t + 1))
                    V.tensor_tensor(p_x[:, t], p_x[:, t], r.unsqueeze(2).to_broadcast([P, XH, SEQ]), ALU.mult).then_inc(xp_ready, 1)
                for t in range(NT):
                    dve.wait_ge(xt2_done, l * 4 + (2 * t + 2))
                    V.tensor_copy(pt_x[:, :, 2:4, t * P:(t + 1) * P],
                                  bank(5 + 2 * t).rearrange("p (m h t) -> p m h t", m=2, h=2)).then_inc(pt2_ready, 1)
                for i in range(4):
                    dve.wait_ge(ox_hi, l * 4 + (i + 1))
                    V.tensor_tensor(loA[:, 2 * i:2 * i + 2, :], bank(i).rearrange("p (c t) -> p c t", c=2), f32(hiA[:, 2 * i:2 * i + 2, :]),
                                    ALU.subtract).then_inc(ox_lo, 1)
                for hf in range(2):
                    for t in range(NT):
                        dve.wait_ge(cross_out, l * 4 + (2 * hf + t + 1))
                        ins = add(4 + 2 * hf + t, t, hf)
                ins.then_inc(x_ready, 1)
                norm_scale(x, l * 4 + 4)
                norm_lo(l, 3, "g_ffn", hiB, loB)

                with dve.If(l < 1):
                    def flo(kind, t):
                        lo(kind, t + ((LAYER_SPLITS if kind < 2 else 0) + 1), 2048)

                    def dense(t, last=False):
                        if not last:
                            flo(0, t + 1)
                        flo(2, t)
                        dve.wait_ge(f_silu, t + 1)
                        dve.wait_ge(w_used[1], t + 1)
                        V.tensor_tensor(f_act[:], f_sil[:], bank(1), ALU.mult).then_inc(f_mul, 1)
                        dve.wait_ge(f_hi_s, t + 1)
                        V.tensor_tensor(f_lo[:], f_act[:].rearrange("p (c t) -> p c t", c=2), f32(f_hi[:]), ALU.subtract).then_inc(f_lo_s, 1)
                        if not last:
                            flo(1, t + 1)

                    flo(0, 0)
                    flo(1, 0)
                    with dve.Fori(0, FF_STEPS - 1) as t:
                        dense(t)
                    dense(FF_STEPS - 1, last=True)
                    dve.wait_ge(w_used[2], FF_STEPS)
                    for hf in range(2):
                        for t in range(NT):
                            ins = add(4 + 2 * t + hf, t, hf)
                    ins.then_inc(x_ready, 1)

            n_rv = [0]

            def step(ins):
                ins.then_inc(rv, 1)
                n_rv[0] += 1
                dve.wait_ge(rv, n_rv[0])

            lg = rt[:, 0:16].rearrange("p (t e) -> p t e", t=NT)
            gt = rt[:, 16:144].rearrange("p (t e j) -> p t e j", t=NT, e=E)
            rank = rt[:, 144:160].rearrange("p (t e) -> p t e", t=NT)
            m0, m1 = (rt[:, a:a + 16].rearrange("p (t e) -> p t e", t=NT) for a in (160, 176))
            w0, w1_ = (rt[:, a:a + 16].rearrange("p (t e) -> p t e", t=NT) for a in (192, 208))
            member = rt[:, 240:256].rearrange("p (t e) -> p t e", t=NT)
            eq = rt[:, 384:512].rearrange("p (t e j) -> p t e j", t=NT, e=E)
            jlt = cst("jlt").rearrange("p (e j) -> p e j", e=E)
            v1, v2, dif, ex = rt[:, 256:258], rt[:, 262:264], rt[:, 258:260], rt[:, 260:262]
            dve.wait_ge(lg_done, 1)
            V.memset(ones[:], 1.0)
            V.memset(keys[:], -1.0)
            V.memset(combs[:], 0.0)
            V.memset(items_f[:], 0.0)
            step(V.tensor_copy(lg, bank(0)[:, 0:16].rearrange("p (t e) -> p t e", t=NT)))
            for t in range(NT):
                lj = lg[:, t].unsqueeze(1).to_broadcast([P, E, E])
                le = lg[:, t].unsqueeze(2).to_broadcast([P, E, E])
                V.tensor_tensor(gt[:, t], lj, le, ALU.is_gt)
                ins = V.tensor_tensor(eq[:, t], lj, le, ALU.is_equal)
            step(ins)
            for t in range(NT):
                ins = V.tensor_tensor(eq[:, t], eq[:, t], jlt, ALU.mult)
            step(ins)
            step(V.tensor_tensor(rt[:, 16:144], rt[:, 16:144], rt[:, 384:512], ALU.add))
            step(V.tensor_reduce(rt[:, 144:160], rt[:, 16:144].rearrange("p (r j) -> p r j", j=E), AX, ALU.add))
            V.tensor_scalar(rt[:, 160:176], rt[:, 144:160], 0.0, None, ALU.is_equal)
            step(V.tensor_scalar(rt[:, 176:192], rt[:, 144:160], 1.0, None, ALU.is_equal))
            V.tensor_tensor(rt[:, 192:208], rt[:, 160:176], rt[:, 0:16], ALU.mult)
            V.tensor_tensor(rt[:, 208:224], rt[:, 176:192], rt[:, 0:16], ALU.mult)
            step(V.tensor_tensor(rt[:, 240:256], rt[:, 160:176], rt[:, 176:192], ALU.add))
            V.tensor_reduce(v1, w0, AX, ALU.add)
            step(V.tensor_reduce(v2, w1_, AX, ALU.add))
            step(V.tensor_tensor(dif, v2, v1, ALU.subtract))
            dve.wait_ge(r_exp, 1)
            gsum, g1, g2 = rt[:, 264:266], rt[:, 266:268], rt[:, 268:270]
            step(V.tensor_scalar(gsum, ex, 1.0, None, ALU.add))
            step(V.reciprocal(g1, gsum))
            step(V.tensor_tensor(g2, g1, ex, ALU.mult))
            V.tensor_tensor(w0, m0, g1.unsqueeze(2).to_broadcast([P, NT, E]), ALU.mult)
            step(V.tensor_tensor(w1_, m1, g2.unsqueeze(2).to_broadcast([P, NT, E]), ALU.mult))
            V.tensor_tensor(combs[:, :, 0:E], w0, w1_, ALU.add)
            dve.wait_ge(pos_done, 1)
            k1 = rt[:, 272:288]
            step(V.scalar_tensor_tensor(out=k1, in0=bank(1)[:, 0:16], scalar=1.0, in1=rt[:, 240:256], op0=ALU.add, op1=ALU.mult))
            step(V.tensor_scalar(keys[:, :, 0:E], k1.rearrange("p (t e) -> p t e", t=NT), -1.0, None, ALU.add))

            def onehots(it):
                for t in range(NT):
                    ins = V.tensor_scalar(onehot[:, t, :], cst("iota", 0, CAP), keys[:, t, bass.ds(it, 1)], None, ALU.is_equal)
                ins.then_inc(oh_ready, 1)
                for t in range(NT):
                    ins = V.tensor_scalar(onehot_g[:, t, :], cst("iota", 0, CAP), keys[:, t, bass.ds(it, 1)], combs[:, t, bass.ds(it, 1)],
                                          ALU.is_equal, ALU.mult)
                ins.then_inc(oh_g_ready, 1)

            onehots(0)
            ov, orank = rt[:, 288:296], rt[:, 296:304]
            sel = rt[:, 512:576].rearrange("p (j e) -> p j e", e=E)
            tmp = rt[:, 576:640].rearrange("p (j e) -> p j e", e=E)
            iota8 = cst("iota", 0, E)
            step(V.tensor_scalar(ov, bank(1)[:, 16:24], float(CAP), None, ALU.is_gt))
            step(V.tensor_tensor(tmp, jlt, ov.unsqueeze(1).to_broadcast([P, E, E]), ALU.mult))
            step(V.tensor_reduce(orank, tmp, AX, ALU.add))
            step(V.tensor_tensor(sel, orank.unsqueeze(1).to_broadcast([P, E, E]), iota8.unsqueeze(2).to_broadcast([P, E, E]), ALU.is_equal))
            step(V.tensor_tensor(sel, sel, ov.unsqueeze(1).to_broadcast([P, E, E]), ALU.mult))
            k2 = rt[:, 304:320].rearrange("p (t e) -> p t e", t=NT)
            step(V.tensor_scalar(k2, keys[:, :, 0:E], -float(CAP), None, ALU.add))
            for t in range(NT):
                for src, dst in ((k2[:, t], keys), (combs[:, t, 0:E], combs)):
                    step(V.tensor_tensor(tmp, sel, src.unsqueeze(1).to_broadcast([P, E, E]), ALU.mult))
                    step(V.tensor_reduce(dst[:, t, E:2 * E], tmp, AX, ALU.add))
            step(V.tensor_tensor(tmp, sel, iota8.unsqueeze(1).to_broadcast([P, E, E]), ALU.mult))
            V.tensor_reduce(items_f[:, E:2 * E], tmp, AX, ALU.add)
            V.tensor_copy(items_f[:, 0:E], iota8)
            step(V.tensor_reduce(rt[:, 320:321], ov, AX, ALU.add))
            step(V.tensor_scalar(items_f[:, NCOL:NCOL + 1], rt[:, 320:321], float(E), None, ALU.add))
            V.tensor_copy(items_i[:], items_f[:]).then_inc(items_ready, 1)

            def mlo(kind, n):
                lo(kind, n + (MOE_SPLITS[kind] + 1))

            def multiply(n):
                dve.wait_ge(m_silu, n)
                dve.wait_ge(w_used[1], n + FF_STEPS)
                V.tensor_tensor(hid_tok[:, 1, :], hid_tok[:, 0, :], bank(1), ALU.mult).then_inc(m_mul, 1)

            def act_lo(n):
                dve.wait_ge(ma_hi, n)
                V.tensor_tensor(a_lo[:], bank(4), f32(a_hi[:]), ALU.subtract).then_inc(ma_lo, 1)

            def scatter_add(it, j):
                t, hf = divmod(j, 2)
                dve.wait_ge(sc_done, it * 4 + (j + 1))
                xv = x[:, t, hf * 512:(hf + 1) * 512]
                return V.tensor_tensor(xv, xv, bank(5), ALU.add).then_inc(sc_add, 1)

            def item(it, first=False):
                for s in range(MOE_STEPS):
                    n = it * MOE_STEPS + s
                    begin = first and s == 0
                    mlo(0, n)
                    if s == 0:
                        dve.wait_ge(e_hi_s, it + 1)
                        for k in range(KD):
                            ins = V.scalar_tensor_tensor(out=e_lo[:, k, :], in0=bank(6 + k // 4)[:, (k % 4) * P:(k % 4) * P + P],
                                                         scalar=sml("g_ffn", k, k + 1), in1=f32(e_hi[:, k, :]), op0=ALU.mult, op1=ALU.subtract)
                        ins.then_inc(e_lo_s, 1)
                    if not begin:
                        multiply(n)
                    mlo(1, n)
                    if s == 1 and not first:
                        dve.wait_ge(w_used[2], it * MOE_STEPS + FF_STEPS)
                        V.tensor_copy(down_out[:, 512:1024], bank(3)).then_inc(md_ev, 1)
                    if not begin:
                        mlo(2, n - 1)
                        act_lo(n)
                    if 2 <= s <= 5 and not first:
                        scatter_add(it, s - 2)
                    if s == MOE_STEPS - 1:
                        dve.wait_ge(gath_done, it + 1)
                        dve.wait_ge(ohT_done, it + 1)
                        onehots(it + 1)

            item(0, first=True)
            n_items = dve.value_load(items_i[0:1, NCOL:NCOL + 1], min_val=E, max_val=2 * E)
            with dve.Fori(1, n_items) as it:
                item(it)
            last = n_items * MOE_STEPS
            multiply(last)
            mlo(2, last - 1)
            act_lo(last)
            dve.wait_ge(w_used[2], n_items * MOE_STEPS + FF_STEPS)
            V.tensor_copy(down_out[:, 512:1024], bank(3)).then_inc(md_ev, 1)
            for j in range(4):
                ins = scatter_add(n_items, j)
            dve.wait_ge(sc_add, n_items * 4 + 4)
            V.memset(stat[:, 56:57], 0.0).then_inc(x_ready, 1)
            dve.wait_ge(ssq_done, DEPTH * 4 + 1)
            V.tensor_scalar(stat[:, 4:6], stat[:, 0:2], 1.0 / D, EPS, ALU.mult, ALU.add).then_inc(ms_done, 1)
            dve.wait_ge(rstd_done, DEPTH * 4 + 1)
            dve.wait_ge(gfin_in, 16)
            for t in range(NT):
                V.scalar_tensor_tensor(out=xs[:, t, :], in0=x[:, t, :], scalar=stat[:, 6 + t:7 + t], in1=gfin[:],
                                       op0=ALU.mult, op1=ALU.mult).then_inc(fin_ready, 1)


def layouts(inputs):
    a = {k: np.asarray(v) for k, v in inputs.items()}
    f = np.float32
    o1, o2, o3 = NSA_W, NSA_W + 6 * 128, NSA_W + 6 * 128 + 24
    q = np.arange(o1).reshape(2, 4, HD).transpose(1, 0, 2).ravel()
    kv = lambda i: np.arange(o1 + i * 128, o1 + (i + 1) * 128)
    cols = np.concatenate([q, kv(2), kv(4), kv(0), kv(1), kv(3), kv(5), np.arange(o2, o3), np.arange(o3, IN_W)])

    def by_cols(w, n):
        r, c = w.shape
        return w.reshape(r // P, P, c // n, n).transpose(2, 1, 0, 3).reshape(c // n, P, r // P * n)

    def by_rows(w, n):
        r, c = w.shape
        return w.reshape(r // n, n // P, P, c).transpose(0, 2, 1, 3).reshape(r // n, P, n // P * c)

    wl = np.zeros((DEPTH, 16, P, 4096), f)
    for l in range(DEPTH):
        wl[l, 0:4, :, :KD * ZW] = by_cols(a["w_in"][l][:, cols], ZW)
        wl[l, 4:5] = by_rows(a["cmp_w1_k"][l], CMP_LEN * HD)
        wl[l, 5:6] = by_rows(a["cmp_w1_v"][l], CMP_LEN * HD)
        for i, n in ((6, "w_out"), (8, "wk_x"), (10, "wv_x"), (12, "wq_x"), (14, "wo_x")):
            wl[l, i:i + 2] = by_cols(a[n][l], 512)
    wf = np.stack([by_cols(a["ffn_wg"][0], FF_STEP), by_cols(a["ffn_wu"][0], FF_STEP), by_rows(a["ffn_wd"][0], FF_STEP)], axis=1)
    wm = np.empty((E, MOE_STEPS, 3, P, 4096), f)
    for e in range(E):
        wm[e, :, 0] = by_cols(a["moe_wg"][0, e], MOE_STEP)
        wm[e, :, 1] = by_cols(a["moe_wu"][0, e], MOE_STEP)
        wm[e, :, 2] = by_rows(a["moe_wd"][0, e], MOE_STEP)
    small = np.zeros((DEPTH, P, SMALL_W), f)

    def put(n, v):
        o, w = SMALL[n]
        small[:, :, o:o + w] = v.reshape(DEPTH, P, w)

    col = lambda v, k: v.reshape(DEPTH, k, P).transpose(0, 2, 1)
    for n, s in (("g_mix", "norm_mix"), ("g_mem", "norm_mem"), ("g_x", "norm_x"), ("g_ffn", "norm_ffn")):
        put(n, col(a[s], KD))
    put("pool_scale", col(a["pool_scale"], 4))
    put("b1", np.concatenate([col(a["cmp_b1_k"], 2), col(a["cmp_b1_v"], 2)], axis=2))
    put("pe", np.concatenate([col(a["cmp_pe_k"], CMP_J), col(a["cmp_pe_v"], CMP_J)], axis=2))
    for n, s in (("w2k", "cmp_w2_k"), ("w2v", "cmp_w2_v")):
        put(n, a[s].reshape(DEPTH, 2, P, HD).transpose(0, 2, 1, 3))
    put("w_pool", a["w_pool"].transpose(0, 2, 1, 3))
    router = a["moe_router"][0].reshape(KD, P, E).transpose(1, 0, 2).reshape(P, KD * E)
    return {"x": a["x"][0], "mem": a["mem"][0], "wl": wl, "wf": wf, "wm": wm, "small": small, "const": constants(),
            "router": router, "gfin": a["norm_final"]}


def constants():
    f = np.float32
    c = np.zeros((P, CONST_W), f)

    def put(n, v):
        o, w = CONST[n]
        c[:, o:o + w] = np.broadcast_to(v, (P, w))

    r = np.arange(P)
    put("ident", np.eye(P, dtype=f))
    put("below", (r[:, None] < r[None, :]).astype(f))
    put("iota", r.astype(f))
    put("jlt", (np.arange(E)[None, :] < np.arange(E)[:, None]).astype(f).ravel())
    half = ROPE // 2
    inv = f(500000.0) ** (-np.arange(half, dtype=f) / f(half))
    ang = np.arange(SEQ, dtype=f)[:, None] * inv[None, :]
    for n, fn in (("cos", np.cos), ("sin", np.sin)):
        v = fn(ang.astype(np.float64)).astype(f)
        v = np.concatenate([v, v], axis=1).reshape(NT, P, ROPE).transpose(1, 0, 2).reshape(P, NT * ROPE)
        put(n, v)
    tok = np.arange(SEQ).reshape(NT, P)
    end = np.append(np.arange(N_CMP) * CMP_STRIDE + CMP_LEN - 1, 10 ** 6)
    m = np.where(end[None, None, :] <= tok[:, :, None], 0.0, NEG).astype(f)
    put("cmp_mask", np.broadcast_to(m.transpose(1, 0, 2)[:, :, None, :], (P, NT, GRP, 16)).reshape(P, 128))
    band = np.zeros((4, SEQ, SEQ), f)
    s = np.arange(SEQ)
    for g, w in enumerate((2, 4, 8, 16)):
        inside = (s[:, None] <= s[None, :]) & (s[:, None] > s[None, :] - w)
        band[g] = inside / np.minimum(s + 1, w)[None, :].astype(f) - np.eye(SEQ, dtype=f)
    put("band", np.concatenate([band[:, :P, :], band[:, P:, P:]], axis=2).transpose(1, 0, 2).reshape(P, 4 * 384))
    put("causal", np.concatenate([np.zeros((P, P), f), np.where(r[None, :] <= r[:, None], 0.0, NEG).astype(f)], axis=1))
    return c


def kernel(**inputs):
    import concourse.bacc as bacc
    from concourse.bass_utils import run_bass_kernel_spmd

    nc = bacc.Bacc("TRN2", target_bir_lowering=False, num_devices=1)
    arrays, args = {}, []
    for name, v in layouts(inputs).items():
        v = np.ascontiguousarray(v)
        arrays[f"{name}_dram"] = v
        args.append(nc.dram_tensor(f"{name}_dram", v.shape, mybir.dt.from_np(v.dtype), kind="ExternalInput").ap())
    args.append(nc.dram_tensor("out_dram", (SEQ, D), F32, kind="ExternalOutput").ap())
    build(nc, *args)
    r = run_bass_kernel_spmd(nc, [arrays], core_ids=[0])
    return r.results[0]["out_dram"].reshape(1, SEQ, D)
```

```python
from contextlib import ExitStack

import numpy as np

import concourse.bass as bass
from concourse import mybir

F32 = mybir.dt.float32
F32R = mybir.dt.float32r
BF16 = mybir.dt.bfloat16
I32 = mybir.dt.int32
ALU = mybir.AluOpType
ACT = mybir.ActivationFunctionType
AX = mybir.AxisListType.X

P = 128
DEPTH, SEQ, D = 2, 256, 1024
NT = SEQ // P
KD = D // P
HEADS, HD, GRP = 8, 64, 4
NSA_W, POOL_W, IN_W = 512, 512, 1816
CMP_LEN, CMP_STRIDE, N_CMP = 32, 16, 15
CMP_J = CMP_LEN * HD // P
ROPE = 16
XH = 4
FF_STEP, FF_STEPS = 256, 11
E, MOE_STEP, MOE_STEPS = 8, 512, 7
CAP = 128
NCOL = 17
ZW = IN_W // 4
EPS = 1e-6
NEG = -1e30

Z_KSLC, Z_KWIN, Z_KCMP, Z_VCMP, Z_VSLC, Z_VWIN, Z_GATE, Z_U = 512, 640, 768, 896, 1024, 1152, 1280, 1304

SMALL = {}
_o = 0
for _n, _w in (("g_mix", 8), ("g_mem", 8), ("g_x", 8), ("g_ffn", 8), ("pool_scale", 4), ("b1", 4), ("pe", 32),
               ("w2k", 128), ("w2v", 128), ("w_pool", 512)):
    SMALL[_n] = (_o, _w)
    _o += _w
SMALL_W = _o
CONST = {}
_o = 0
for _n, _w in (("band", 4 * 384), ("ident", 128), ("below", 128), ("iota", 128), ("jlt", 64), ("cos", 32), ("sin", 32),
               ("cmp_mask", 128), ("causal", 256)):
    CONST[_n] = (_o, _w)
    _o += _w
CONST_W = _o
CONST_KEEP = CONST["causal"][0]

LAYER_SPLITS = 7
LAYER_LOADS = 8
PER_LAYER_SPLITS = LAYER_SPLITS + FF_STEPS
PER_LAYER_LOADS = LAYER_LOADS + FF_STEPS
MOE_SPLITS = (2 * LAYER_SPLITS + FF_STEPS,) * 2 + (FF_STEPS,)
MOE_LOADS = (2 * LAYER_LOADS + FF_STEPS,) * 2 + (FF_STEPS,)


def build(nc, x_d, mem_d, wl_d, wf_d, wm_d, small_d, const_d, router_d, gfin_d, out_d):
    ctx = ExitStack()
    with ctx:
        base = 16512

        def at(name, off, shape, dt=F32):
            return nc.alloc_sbuf_tensor_at(name, [P] + shape, dt, offset=base + off)

        def sem(name):
            return ctx.enter_context(nc.semaphore(name))

        K = 1024
        x = at("x", 0, [NT, D])
        xs = at("xs", 8 * K, [NT, D])
        hiA, loA = at("hiA", 16 * K, [KD, SEQ], F32R), at("loA", 24 * K, [KD, SEQ], F32R)
        hiB, loB = at("hiB", 32 * K, [KD, SEQ], F32R), at("loB", 40 * K, [KD, SEQ], F32R)
        stage = [at(f"stage{i}", 48 * K + (i * 48 if i < 2 else 96) * K, [4096]) for i in range(3)]
        whi = [at(f"whi{i}", 64 * K + (i * 48 if i < 2 else 96) * K, [4096], F32R) for i in range(3)]
        wlo = [at(f"wlo{i}", 80 * K + (i * 48 if i < 2 else 96) * K, [4096], F32R) for i in range(3)]
        T = 144 * K
        z = at("z", T, [NT, IN_W])
        qk_rot = at("qk_rot", T + 14592, [NT, 768])
        q_raw_T = at("q_raw_T", T + 20736, [4, SEQ])
        q_rot_T = at("q_rot_T", T + 24832, [4, SEQ])
        k_T = at("k_T", T + 28928, [2, SEQ])
        probs = [at("probs0", T + 30976, [2048]), at("probs1", T + 39168, [2048])]
        rope_c = at("rope_c", T + 30976, [NT, 12, ROPE])
        rope_s = at("rope_s", T + 30976 + 1536, [NT, 12, ROPE])
        blk_T = at("blk_T", T + 39168, [2, CMP_J, 2 * N_CMP])
        d_T = at("d_T", T + 39168 + 3840, [4, SEQ])
        pt = [at(f"pt{i}", T + 14592 + 2048 * i, [512]) for i in range(2)]
        cmask_f = at("cmask_f", T + 39168, [256])
        kx_T, v_x, q_x_T = at("kx_T", T, [8, SEQ]), at("v_x", T + 8 * K, [NT, D]), at("q_x_T", T + 16 * K, [8, SEQ])
        p_x = at("p_x", T + 24 * K, [NT, XH, SEQ])
        pt_x = at("pt_x", T + 32 * K, [NT, XH, SEQ])
        C = 192 * K
        small = at("small", C, [SMALL_W])
        const = at("const", C + 3360, [CONST_KEEP])
        o = C + 3360 + 4 * CONST_KEEP
        router = at("router", o, [KD, E]); o += 256
        ident_bf = at("ident_bf", o, [P], BF16); o += 256
        causal_bf = at("causal_bf", o, [256], BF16); o += 512
        stat = at("stat", o, [80]); o += 320
        gates = at("gates", o, [NT, 24]); o += 192
        k_cmp_T = at("k_cmp_T", o, [16]); o += 64
        v_bd = at("v_bd", o, [2, 256]); o += 2048
        hid = at("hid", T + 48384, [2, 2, 2 * N_CMP])
        hid_pre = z[0:2 * N_CMP, 0, 0:512]
        MOE = 32 * K
        hid_tok = at("hid_tok", MOE, [2, MOE_STEP])
        a_hi, a_lo = at("a_hi", MOE + 4096, [512], F32R), at("a_lo", MOE + 6144, [512], F32R)
        down_hi, down_lo = at("down_hi", MOE + 8192, [D], F32R), at("down_lo", MOE + 12288, [D], F32R)
        onehot, onehot_T = at("onehot", 29 * K + 512, [NT, CAP], F32R), at("onehot_T", 30 * K + 512, [SEQ], F32R)
        xs_hi, xs_lo = at("xs_hi", C + 1312, [NT, D], F32R), at("xs_lo", 8 * K, [NT, D], F32R)
        gate_tok, gate_slot = stat[:, 60:62], stat[:, 62:63]
        f_sil, f_act = at("f_sil", 16 * K, [512]), at("f_act", 18 * K, [512])
        f_hi, f_lo = at("f_hi", 20 * K, [2, SEQ], F32R), at("f_lo", 22 * K, [2, SEQ], F32R)
        e_hi, e_lo = at("e_hi", 16 * K, [KD, CAP], F32R), at("e_lo", 20 * K, [KD, CAP], F32R)
        p_cmp = at("p_cmp", T + 18688, [16, 32])
        l_cmp = at("l_cmp", T + 47360, [16, 16])
        rt = at("rt", 24 * K, [1024])
        keys = at("keys", 28 * K, [NT, NCOL])
        combs = at("combs", 28 * K + 256, [NT, NCOL])
        items_i = at("items_i", 28 * K + 512, [NCOL + 1], I32)
        items_f = at("items_f", 28 * K + 640, [NCOL + 1])
        ones = at("ones", 29 * K, [P])
        gfin = at("gfin", 24 * K, [D])
        lg_T = at("lg_T", 26 * K + 512, [SEQ])[0:E, :]
        router_hi, router_lo = at("router_hi", 27 * K, [KD, E], F32R), at("router_lo", 27 * K + 256, [KD, E], F32R)
        junk = at("junk", T + 35072, [NT, D], BF16)
        assert base + o <= 229344, o

        PS = ctx.enter_context(nc.psum_tensor("PS", [P, 8, 512], F32))

        def bank(i):
            return PS[:, i, :]

        def cst(n, a=0, b=None):
            off, w = CONST[n]
            return const[:, off + a:off + (w if b is None else b)]

        def sml(n, a=0, b=None):
            off, w = SMALL[n]
            return small[:, off + a:off + (w if b is None else b)]

        ident = cst("ident")
        f32 = lambda ap: ap.bitcast(F32)

        x_in, const_in, small_in, mem_in = sem("x_in"), sem("const_in"), sem("small_in"), sem("mem_in")
        mask_in, router_in, gfin_in, out_done = sem("mask_in"), sem("router_in"), sem("gfin_in"), sem("out_done")
        consts_ready = sem("consts_ready")
        w_in_ring = [sem(f"w_landed{i}") for i in range(3)]
        w_hi = [sem(f"w_hi{i}") for i in range(3)]
        w_lo = [sem(f"w_lo{i}") for i in range(3)]
        w_used = [sem(f"w_used{i}") for i in range(3)]
        x_ready = sem("x_ready")
        ssq_done, ms_done, rstd_done, xs_ready = sem("ssq_done"), sem("ms_done"), sem("rstd_done"), sem("xs_ready")
        xT_done, n_hi, n_lo = sem("xT_done"), sem("n_hi"), sem("n_lo")
        z_done, z_act, z_dve = sem("z_done"), sem("z_act"), sem("z_dve")
        qk_copied, rope_done, rope_part = sem("qk_copied"), sem("rope_done"), sem("rope_part")
        tq_done, xt_done, tr_done, pd_done = sem("tq_done"), sem("xt_done"), sem("tr_done"), sem("pd_done")
        q_rot_ready, q_raw_ready, d_ready = sem("q_rot_ready"), sem("q_raw_ready"), sem("d_ready")
        blk_ready, hid_done, hid_copied, hidT_done, gelu_done = (sem("blk_ready"), sem("hid_done"), sem("hid_copied"),
                                                                 sem("hidT_done"), sem("gelu_done"))
        y_done, y_hi, y_lo = sem("y_done"), sem("y_hi"), sem("y_lo")
        kcvc_done, kcvc_ready, cs_done = sem("kcvc_done"), sem("kcvc_ready"), sem("cs_done")
        gate_e, gate_v = sem("gate_e"), sem("gate_v")
        cmp_v, cmp_e, pc_ready, p_cmp_zero = sem("cmp_v"), sem("cmp_e"), sem("pc_ready"), sem("p_cmp_zero")
        s_done, max_done, nm_ready, exps_done, r_done, p_ready = (sem("s_done"), sem("max_done"), sem("nm_ready"),
                                                                  sem("exps_done"), sem("r_done"), sem("p_ready"))
        t_done, pt_act, pt_dve, pv_done = sem("t_done"), sem("pt_act"), sem("pt_dve"), sem("pv_done")
        cc_hi, cc_lo = sem("cc_hi"), sem("cc_lo")
        mix_out, mix_add = sem("mix_out"), sem("mix_add")
        kvq_done, kvq_act, kvq_dve = sem("kvq_done"), sem("kvq_act"), sem("kvq_dve")
        xs_done, xmax_done, xnm_ready, xexp_done, xr_done, xp_ready = (sem("xs_done"), sem("xmax_done"), sem("xnm_ready"),
                                                                       sem("xexp_done"), sem("xr_done"), sem("xp_ready"))
        xt2_done, pt2_ready = sem("xt2_done"), sem("pt2_ready")
        ox_done, ox_hi, ox_lo, cross_out = sem("ox_done"), sem("ox_hi"), sem("ox_lo"), sem("cross_out")
        f_silu, f_mul, f_hi_s, f_lo_s = sem("f_silu"), sem("f_mul"), sem("f_hi_s"), sem("f_lo_s")
        router_parts, lg_done, rv, r_exp, pos_done, items_ready = (sem("router_parts"), sem("lg_done"), sem("rv"), sem("r_exp"),
                                                                   sem("pos_done"), sem("items_ready"))
        xg_hi, xg_lo, lgT_ready = sem("xg_hi"), sem("xg_lo"), sem("lgT_ready")
        oh_ready, gath_done, e_hi_s, e_lo_s = sem("oh_ready"), sem("gath_done"), sem("e_hi_s"), sem("e_lo_s")
        m_silu, m_mul, mt_done, ma_hi, ma_lo = sem("m_silu"), sem("m_mul"), sem("mt_done"), sem("ma_hi"), sem("ma_lo")
        md_hi, md_lo, ohT_done, ohT_ready, sc_done, sc_add = (sem("md_hi"), sem("md_lo"), sem("ohT_done"),
                                                              sem("ohT_ready"), sem("sc_done"), sem("sc_add"))
        last_in, fin_ready = sem("last_in"), sem("fin_ready")

        block = ctx.enter_context(nc.Block())

        @block.sync
        def _(sp):
            sp.dma_start(x[:], x_d.rearrange("(t p) d -> p t d", p=P)).then_inc(x_in, 16)
            sp.dma_start(const[:], const_d[:, 0:CONST_KEEP]).then_inc(const_in, 16)
            sp.dma_start(cmask_f[:], const_d[:, CONST_KEEP:CONST_W]).then_inc(mask_in, 16)
            sp.dma_start(router[:].rearrange("p k e -> p (k e)"), router_d).then_inc(router_in, 16)

            with sp.Fori(0, DEPTH) as l:
                for i in range(16):
                    slot = i % 2
                    if i - 2 in (4, 5):
                        sp.wait_ge(hid_done, l * 2 + (i - 2 - 3))
                    elif i >= 2:
                        split = i - 2 if i - 2 < 4 else i - 4
                        sp.wait_ge(w_lo[slot], l * PER_LAYER_SPLITS + (split // 2 + 1))
                    n = KD * ZW if i < 4 else 4096
                    sp.dma_start(stage[slot][:, 0:n], wl_d[bass.ds(l, 1), i, :, 0:n].rearrange("o p n -> p (o n)")) \
                        .then_inc(w_in_ring[slot], 16)
                with sp.If(l < 1):
                    def load(t, kind):
                        sp.dma_start(stage[kind][:, 0:2048], wf_d[bass.ds(t, 1), kind, :, :].rearrange("o p n -> p (o n)")) \
                            .then_inc(w_in_ring[kind], 16)

                    sp.wait_ge(w_lo[0], LAYER_SPLITS)
                    load(0, 0)
                    sp.wait_ge(w_lo[1], LAYER_SPLITS)
                    load(0, 1)
                    sp.wait_ge(w_lo[0], LAYER_SPLITS + 1)
                    load(1, 0)
                    sp.wait_ge(ox_done, 4)
                    load(0, 2)
                    sp.wait_ge(w_lo[1], LAYER_SPLITS + 1)
                    load(1, 1)
                    with sp.Fori(1, FF_STEPS - 1) as t:
                        sp.wait_ge(w_lo[0], t + (LAYER_SPLITS + 1))
                        load(t + 1, 0)
                        sp.wait_ge(w_lo[2], t + 0)
                        load(t, 2)
                        sp.wait_ge(w_lo[1], t + (LAYER_SPLITS + 1))
                        load(t + 1, 1)
                    sp.wait_ge(w_lo[2], FF_STEPS - 1)
                    load(FF_STEPS - 1, 2)
                    for slot in range(2):
                        sp.wait_ge(w_lo[slot], LAYER_SPLITS + FF_STEPS)

            def load_e(e, s, kind):
                sp.dma_start(stage[kind][:], wm_d[bass.ds(e, 1), s, kind, :, :].rearrange("o p n -> p (o n)")) \
                    .then_inc(w_in_ring[kind], 16)

            def load_item(it, e, e_before, first=False):
                for s in range(MOE_STEPS):
                    n = it * MOE_STEPS + s
                    sp.wait_ge(w_lo[0], n + MOE_SPLITS[0])
                    load_e(e, s, 0)
                    sp.wait_ge(w_lo[1], n + MOE_SPLITS[1])
                    load_e(e, s, 1)
                    if first and s == 0:
                        continue
                    if first and s == 1:
                        sp.wait_ge(ox_done, 4 * DEPTH)
                    sp.wait_ge(w_lo[2], n + (MOE_SPLITS[2] - 1))
                    load_e(e if s else e_before, (s - 1) % MOE_STEPS, 2)

            load_item(0, 0, 0, first=True)
            with sp.Fori(1, E) as it:
                load_item(it, it, it - 1)
            sp.wait_ge(items_ready, 1)
            n_items = sp.value_load(items_i[0:1, NCOL:NCOL + 1], min_val=E, max_val=2 * E)
            with sp.If(n_items > E):
                with sp.Fori(E, n_items) as it:
                    e = sp.value_load(items_i[0:1, bass.ds(it, 1)], min_val=0, max_val=E - 1)
                    eb = sp.value_load(items_i[0:1, bass.ds(it - 1, 1)], min_val=0, max_val=E - 1)
                    load_item(it, e, eb)
            last = sp.value_load(items_i[0:1, bass.ds(n_items - 1, 1)], min_val=0, max_val=E - 1)
            sp.wait_ge(w_lo[2], n_items * MOE_STEPS + (MOE_SPLITS[2] - 1))
            for h in range(2):
                half = slice(h * 2048, (h + 1) * 2048)
                sp.dma_start(stage[2][:, half], wm_d[bass.ds(last, 1), MOE_STEPS - 1, 2, :, half].rearrange("o p n -> p (o n)")) \
                    .then_inc(last_in if h else w_in_ring[2], 16)
            for t in range(NT):
                sp.wait_ge(fin_ready, t + 1)
                sp.dma_start(out_d[t * P:(t + 1) * P, :], xs[:, t, :]).then_inc(out_done, 16)
            sp.wait_ge(out_done, 16 * NT)

        @block.gpsimd
        def _(pool):
            pool.dma_start(small[:], small_d[0]).then_inc(small_in, 16)
            pool.memset(stat[:, 2:4], -0.5).then_inc(consts_ready, 1)
            pool.memset(v_bd[:], 0.0).then_inc(consts_ready, 1)
            pool.wait_ge(consts_ready, 2)

            def rstd(n):
                pool.wait_ge(ms_done, n)
                nc.gpsimd.tensor_tensor(stat[:, 6:8], stat[:, 4:6], stat[:, 2:4], ALU.pow).then_inc(rstd_done, 1)

            for l in range(DEPTH):
                rstd(l * 4 + 1)
                pool.wait_ge(xT_done, l * 16 + 4)
                pool.dma_start(xs[:], mem_d.rearrange("(t p) d -> p t d", p=P)).then_inc(mem_in, 16)
                rstd(l * 4 + 2)
                pool.wait_ge(tq_done, l * 3 + 3)
                pool.memset(p_cmp[:], 0.0).then_inc(p_cmp_zero, 1)
                rstd(l * 4 + 3)
                rstd(l * 4 + 4)
                if l < DEPTH - 1:
                    pool.wait_ge(n_hi, (l + 1) * 16)
                    pool.wait_ge(n_lo, (l + 1) * 16)
                    pool.dma_start(small[:], small_d[l + 1]).then_inc(small_in, 16)
            pool.wait_ge(items_ready, 1)
            pool.dma_start(gfin[:], gfin_d.partition_broadcast(P)).then_inc(gfin_in, 16)
            rstd(DEPTH * 4 + 1)
            pool.wait_ge(gfin_in, 16)

        @block.scalar
        def _(act):
            def hi(slot, loads, n=4096):
                act.wait_ge(w_in_ring[slot], loads * 16)
                nc.scalar.activation(whi[slot][:, 0:n], stage[slot][:, 0:n], ACT.Copy).then_inc(w_hi[slot], 1)

            def squares(src, ready=None):
                for t in range(NT):
                    if ready is not None:
                        act.wait_ge(x_ready, ready + (t + 1))
                    ins = nc.scalar.activation(junk[:, t, :], src[:, t, :], ACT.Square, accum_out=stat[:, t:t + 1])
                ins.then_inc(ssq_done, 1)

            def norm_hi(l, j, gain, dst):
                for i in range(4):
                    act.wait_ge(xT_done, l * 16 + (4 * j + i + 1))
                    for k in (2 * i, 2 * i + 1):
                        ins = nc.scalar.activation(dst[:, k, :], bank(i)[:, (k % 2) * 256:(k % 2) * 256 + 256], ACT.Copy,
                                                   scale=sml(gain, k, k + 1))
                    ins.then_inc(n_hi, 1)

            def hi_layer(l, s):
                slot, i = s % 2, (s if s < 4 else s + 2)
                if 2 <= s < 6:
                    act.wait_ge(z_done, l * 8 + 2 * (s - 1))
                elif 6 <= s < 8:
                    act.wait_ge(mix_out, l * 4 + 2 * (s - 5))
                elif s >= 8:
                    act.wait_ge(kvq_done, l * 12 + 2 * (s - 7))
                hi(slot, l * PER_LAYER_LOADS + (i // 2 + 1), KD * ZW if s < 4 else 4096)

            def exps(l, u, tt, slot):
                nk = P * (tt + 1)
                act.wait_ge(nm_ready, l * 4 + (u + 1))
                b0 = 2 if u == 3 else 0
                sc = PS[:, b0:b0 + HEADS * nk // 512, :].rearrange("p b n -> p (b n)")
                for h in range(HEADS):
                    ins = nc.scalar.activation(probs[slot][:, h * nk:(h + 1) * nk], sc[:, h * nk:(h + 1) * nk], ACT.Exp,
                                               bias=stat[:, 16 + 8 * slot + h:17 + 8 * slot + h], scale=HD ** -0.5,
                                               accum_out=stat[:, 32 + 8 * slot + h:33 + 8 * slot + h])
                ins.then_inc(exps_done, 1)

            def pt_even(l, i):
                act.wait_ge(t_done, l * 13 + (i + 1))
                if i >= 2:
                    act.wait_ge(pv_done, l * 13 + (i - 1))
                nc.scalar.activation(pt[0][:], bank(6), ACT.Copy).then_inc(pt_act, 1)

            act.wait_ge(x_in, 16)
            with act.Fori(0, DEPTH) as l:
                squares(x, l * 3 * NT)
                hi_layer(l, 0)
                act.wait_ge(small_in, l * 16 + 16)
                norm_hi(l, 0, "g_mix", hiA)
                hi_layer(l, 1)
                for c in range(4):
                    act.wait_ge(z_done, l * 8 + (2 * c + 1))
                    nc.scalar.activation(z[:, 0, c * ZW:(c + 1) * ZW], bank(4 + 2 * (c % 2))[:, 0:ZW], ACT.Copy).then_inc(z_act, 1)
                    if c == 1:
                        act.wait_ge(z_act, l * 4 + 2)
                        act.wait_ge(z_dve, l * 4 + 2)
                        nc.scalar.activation(qk_rot[:], z[:, :, 0:768], ACT.Copy).then_inc(qk_copied, 1)
                    if c < 2:
                        hi_layer(l, c + 2)
                    if c == 2:
                        act.wait_ge(mem_in, l * 16 + 16)
                        act.wait_ge(ms_done, l * 4 + 1)
                        squares(xs)
                norm_hi(l, 1, "g_mem", hiA)
                act.wait_ge(z_dve, l * 4 + 4)
                act.wait_ge(z_act, l * 4 + 4)
                nc.scalar.activation(gates[:], z[:, :, Z_GATE:Z_GATE + 24], ACT.Exp, scale=-1.0).then_inc(gate_e, 1)
                act.wait_ge(tq_done, l * 3 + 1)
                nc.scalar.activation(q_rot_T[:, 0:2, :], bank(4).rearrange("p (c t) -> p c t", c=2), ACT.Copy).then_inc(q_rot_ready, 1)
                act.wait_ge(tq_done, l * 3 + 3)
                nc.scalar.activation(k_T[:], bank(6).rearrange("p (c t) -> p c t", c=2), ACT.Copy).then_inc(q_rot_ready, 1)
                act.wait_ge(tr_done, l * 2 + 1)
                nc.scalar.activation(q_raw_T[:, 0:2, :], bank(0).rearrange("p (c t) -> p c t", c=2), ACT.Copy).then_inc(q_raw_ready, 1)
                act.wait_ge(pd_done, l * 2 + 1)
                nc.scalar.activation(d_T[:, 0:2, :], bank(2).rearrange("p (c t) -> p c t", c=2), ACT.Copy).then_inc(d_ready, 1)
                exps(l, 0, 1, 0)
                for kv in range(2):
                    act.wait_ge(hid_done, l * 2 + (kv + 1))
                    nc.scalar.activation(hid_pre[:, kv * 256:(kv + 1) * 256], bank(6 + kv)[0:2 * N_CMP, 0:256], ACT.Copy).then_inc(hid_copied, 1)
                act.wait_ge(hidT_done, l + 1)
                for g in range(4):
                    ins = nc.scalar.activation(hid[:, g // 2, g % 2, :], bank(6)[:, g * P:g * P + 2 * N_CMP], ACT.Gelu_apprx_tanh,
                                               bias=sml("b1", g, g + 1))
                ins.then_inc(gelu_done, 1)
                for i in range(2):
                    act.wait_ge(y_done, l * 2 + (i + 1))
                    for g in (2 * i, 2 * i + 1):
                        ins = nc.scalar.activation(hiB[:, 4 + g, :], bank(4 + i)[:, (g % 2) * 256:(g % 2) * 256 + 256], ACT.Copy,
                                                   scale=sml("pool_scale", g, g + 1))
                    ins.then_inc(y_hi, 1)
                hi_layer(l, 4)
                exps(l, 1, 1, 1)
                act.wait_ge(cmp_v, l * 8 + 5)
                nc.scalar.activation(l_cmp[:], l_cmp[:], ACT.Exp).then_inc(cmp_e, 1)
                pt_even(l, 0)
                hi_layer(l, 5)
                pt_even(l, 2)
                pt_even(l, 4)
                exps(l, 2, 0, 0)
                pt_even(l, 6)
                exps(l, 3, 0, 1)
                pt_even(l, 8)
                pt_even(l, 10)
                pt_even(l, 12)
                for i, tt in enumerate((1, 0)):
                    act.wait_ge(pv_done, l * 13 + (9 if tt else 13))
                    nc.scalar.activation(hiB[:, 0:4, tt * P:(tt + 1) * P], bank(4 + tt).rearrange("p (c t) -> p c t", c=4),
                                         ACT.Copy).then_inc(cc_hi, 1)
                hi_layer(l, 6)
                hi_layer(l, 7)
                act.wait_ge(ms_done, l * 4 + 2)
                squares(x, l * 3 * NT + NT)
                dests = [kx_T[:, 0:2, :], kx_T[:, 4:6, :], q_x_T[:, 0:2, :], q_x_T[:, 4:6, :], v_x[:, 0, 0:512], v_x[:, 0, 512:1024]]

                def kvq(i):
                    act.wait_ge(kvq_done, l * 12 + (2 * i + 1))
                    src = bank(4 + 2 * (i % 2))
                    src = src if i >= 4 else src.rearrange("p (c t) -> p c t", c=2)
                    nc.scalar.activation(dests[i], src, ACT.Copy).then_inc(kvq_act, 1)

                kvq(0)
                hi_layer(l, 8)
                norm_hi(l, 2, "g_x", hiB)
                kvq(1)
                hi_layer(l, 9)
                kvq(2)
                hi_layer(l, 10)
                kvq(3)
                hi_layer(l, 11)
                for tt in range(NT):
                    act.wait_ge(xnm_ready, l * 2 + (tt + 1))
                    for h in range(XH):
                        ins = nc.scalar.activation(p_x[:, tt, h, :], bank(2 * tt + h // 2)[:, (h % 2) * 256:(h % 2) * 256 + 256], ACT.Exp,
                                                   bias=stat[:, 16 + 4 * tt + h:17 + 4 * tt + h], scale=256 ** -0.5,
                                                   accum_out=stat[:, 32 + 4 * tt + h:33 + 4 * tt + h])
                    ins.then_inc(xexp_done, 1)
                kvq(4)
                hi_layer(l, 12)
                kvq(5)
                for tt in range(NT):
                    act.wait_ge(xt2_done, l * 4 + (2 * tt + 1))
                    nc.scalar.activation(pt_x[:, :, 0:2, tt * P:(tt + 1) * P],
                                         bank(4 + 2 * tt).rearrange("p (m h t) -> p m h t", m=2, h=2), ACT.Copy).then_inc(pt2_ready, 1)
                hi_layer(l, 13)
                for i in range(4):
                    act.wait_ge(ox_done, l * 4 + (i + 1))
                    nc.scalar.activation(hiA[:, 2 * i:2 * i + 2, :], bank(i).rearrange("p (c t) -> p c t", c=2), ACT.Copy).then_inc(ox_hi, 1)
                act.wait_ge(ms_done, l * 4 + 3)
                squares(x, l * 3 * NT + 2 * NT)
                norm_hi(l, 3, "g_ffn", hiB)

                with act.If(l < 1):
                    def fhi(kind, t, first=False):
                        b_l = LAYER_LOADS if kind < 2 else 0
                        if not first:
                            act.wait_ge(w_used[kind], t)
                        hi(kind, t + (b_l + 1), 2048)

                    def dense(t, first=False, last=False):
                        act.wait_ge(w_used[0], t + 1)
                        if not first:
                            act.wait_ge(f_mul, t + 0)
                        nc.scalar.activation(f_sil[:], bank(0), ACT.Silu).then_inc(f_silu, 1)
                        if not last:
                            fhi(0, t + 1)
                        fhi(2, t + 0, first)
                        act.wait_ge(f_mul, t + 1)
                        nc.scalar.activation(f_hi[:], f_act[:].rearrange("p (c t) -> p c t", c=2), ACT.Copy).then_inc(f_hi_s, 1)
                        if not last:
                            fhi(1, t + 1)

                    act.wait_ge(cross_out, 4)
                    fhi(0, 0, True)
                    fhi(1, 0, True)
                    dense(0, first=True)
                    with act.Fori(1, FF_STEPS - 1) as t:
                        dense(t)
                    dense(FF_STEPS - 1, last=True)
                    for slot in range(2):
                        act.wait_ge(w_used[slot], FF_STEPS)

            act.wait_ge(router_in, 16)
            nc.scalar.activation(router_hi[:], router[:], ACT.Copy).then_inc(router_parts, 1)
            nc.scalar.activation(xs_hi[:], xs[:], ACT.Copy).then_inc(xg_hi, 1)
            def mhi(kind, n, first=False):
                if not first:
                    act.wait_ge(w_used[kind], n + FF_STEPS)
                hi(kind, n + (MOE_LOADS[kind] + 1))

            def down_parts():
                nc.scalar.activation(down_hi[:].rearrange("p (b n) -> p b n", b=2), PS[:, 2:4, :], ACT.Copy, scale=gate_slot).then_inc(md_hi, 1)

            def item(it, first=False):
                for s in range(MOE_STEPS):
                    n = it * MOE_STEPS + s
                    begin = first and s == 0
                    if not begin:
                        mhi(0, n)
                    if s == 0:
                        act.wait_ge(gath_done, it + 1)
                        for k in range(KD):
                            ins = nc.scalar.activation(e_hi[:, k, :], bank(6 + k // 4)[:, (k % 4) * P:(k % 4) * P + P], ACT.Copy,
                                                       scale=sml("g_ffn", k, k + 1))
                        ins.then_inc(e_hi_s, 1)
                    if not begin:
                        mhi(1, n)
                    if s == 1 and not first:
                        act.wait_ge(w_used[2], it * MOE_STEPS + FF_STEPS)
                        down_parts()
                    if not begin:
                        mhi(2, n - 1, first and s == 1)
                    act.wait_ge(w_used[0], n + (FF_STEPS + 1))
                    if not begin:
                        act.wait_ge(m_mul, n + 0)
                    nc.scalar.activation(hid_tok[:, 0, :], bank(0), ACT.Silu).then_inc(m_silu, 1)
                    if not begin:
                        act.wait_ge(mt_done, n + 0)
                        nc.scalar.activation(a_hi[:], bank(4), ACT.Copy).then_inc(ma_hi, 1)
                    if s == 5:
                        act.wait_ge(ohT_done, it + 1)
                        nc.scalar.activation(gate_slot, bank(6)[:, SEQ:SEQ + 1], ACT.Copy)
                        nc.scalar.activation(onehot_T[:], bank(6)[:, 0:SEQ], ACT.Copy).then_inc(ohT_ready, 1)

            act.wait_ge(cross_out, 4 * DEPTH)
            mhi(0, 0, True)
            mhi(1, 0, True)
            act.wait_ge(rv, 9)
            nc.scalar.activation(rt[:, 260:262], rt[:, 258:260], ACT.Exp).then_inc(r_exp, 1)
            item(0, first=True)
            act.wait_ge(items_ready, 1)
            n_items = act.value_load(items_i[0:1, NCOL:NCOL + 1], min_val=E, max_val=2 * E)
            with act.Fori(1, n_items) as it:
                item(it)
            steps = n_items * MOE_STEPS
            act.wait_ge(w_used[2], steps + (FF_STEPS - 1))
            for h in range(2):
                if h == 0:
                    act.wait_ge(w_in_ring[2], (steps + MOE_LOADS[2]) * 16)
                else:
                    act.wait_ge(last_in, 16)
                half = slice(h * 2048, (h + 1) * 2048)
                nc.scalar.activation(whi[2][:, half], stage[2][:, half], ACT.Copy).then_inc(w_hi[2], 1)
                if h == 0:
                    act.wait_ge(mt_done, steps)
                    nc.scalar.activation(a_hi[:], bank(4), ACT.Copy).then_inc(ma_hi, 1)
            act.wait_ge(w_used[2], n_items * MOE_STEPS + FF_STEPS)
            down_parts()
            squares(x, 3 * NT * DEPTH)

        @block.tensor
        def _(pe):
            mm = nc.tensor.matmul

            def product(out, ah, al, bh, bl, start, stop):
                mm(out, ah, bh, start=start, stop=False)
                mm(out, ah, bl, start=False, stop=False)
                return mm(out, al, bh, start=False, stop=stop)

            def norm_T(l, j):
                pe.wait_ge(xs_ready, l * 4 + (j + 1))
                for i in range(4):
                    for k in (2 * i, 2 * i + 1):
                        for t in range(NT):
                            ins = nc.tensor.transpose(bank(i)[:, (k % 2) * 256 + t * P:(k % 2) * 256 + (t + 1) * P],
                                                      xs[:, t, k * P:(k + 1) * P], ident)
                    ins.then_inc(xT_done, 1)

            def weights(slot, n=512):
                w = slice(0, KD * n)
                return (whi[slot][:, w].rearrange("p (k n) -> p k n", k=KD), wlo[slot][:, w].rearrange("p (k n) -> p k n", k=KD))

            def head(h):
                return slice((h // GRP) * HD, (h // GRP) * HD + HD), h % GRP

            def scores(l, u, br, tt):
                nk, b0 = P * (tt + 1), (2 if u == 3 else 0)
                nb = HEADS * nk // 512
                mask = causal_bf[:, 256 - nk:256]
                for b in range(nb):
                    hb = 512 // nk
                    rows = mask.unsqueeze(1).to_broadcast([P, hb, nk])
                    mm(bank(b0 + b).rearrange("p (h n) -> p h n", h=hb), ident_bf[:], rows, start=True, stop=False,
                       skip_group_check=True)
                for h in range(HEADS):
                    rows, c = head(h)
                    b, o_ = divmod(h * nk, 512)
                    ins = mm(bank(b0 + b)[:, o_:o_ + nk], q_rot_T[rows, c, tt * P:(tt + 1) * P], k_T[rows, br, 0:nk],
                             start=False, stop=True, skip_group_check=True)
                ins.then_inc(s_done, 1)

            units = [(0, 1, 0), (1, 1, 1), (0, 0, 0), (1, 0, 1)]
            groups = []
            for u, (br, tt, slot) in enumerate(units):
                nk = tt + 1
                for gg in range(2):
                    for kc in range(nk):
                        groups.append((u, [(gg * GRP + c, kc) for c in range(GRP)]))
                if u == 0:
                    groups.append(None)

            def transpose_group(l, i):
                g = groups[i]
                if i >= 2:
                    pe.wait_ge(pt_act if i % 2 == 0 else pt_dve, l * (7 if i % 2 == 0 else 6) + i // 2)
                if g is None:
                    pe.wait_ge(pc_ready, l + 1)
                    for q in range(4):
                        ins = nc.tensor.transpose(bank(6 + i % 2)[:, q * P:(q + 1) * P],
                                                  p_cmp[:, 4 * q:4 * q + 4, :].rearrange("p c s -> p (c s)"), ident)
                else:
                    u, tiles = g
                    br, tt, slot = units[u]
                    nk = P * (tt + 1)
                    pe.wait_ge(p_ready, l * 4 + (u + 1))
                    for q, (h, kc) in enumerate(tiles):
                        a = h * nk + kc * P
                        ins = nc.tensor.transpose(bank(6 + i % 2)[:, q * P:(q + 1) * P], probs[slot][:, a:a + P], ident)
                ins.then_inc(t_done, 1)

            def pv_group(l, i):
                g = groups[i]
                pe.wait_ge(pt_act if i % 2 == 0 else pt_dve, l * (7 if i % 2 == 0 else 6) + (i // 2 + 1))
                src = pt[i % 2]
                if g is None:
                    for q in range(4):
                        gg, tt = divmod(q, 2)
                        for c in range(GRP):
                            ins = mm(bank(4 + tt)[gg * HD:(gg + 1) * HD, c * P:(c + 1) * P], v_bd[:, gg, c * HD:(c + 1) * HD],
                                     src[:, q * P:(q + 1) * P], start=(tt == 0 and c == 0), stop=True, skip_group_check=True)
                else:
                    u, tiles = g
                    br, tt, slot = units[u]
                    (h, kc) = tiles[0]
                    gg, v0 = h // GRP, (Z_VSLC if br == 0 else Z_VWIN)
                    ins = mm(bank(4 + tt)[gg * HD:(gg + 1) * HD, :], z[:, kc, v0 + gg * HD:v0 + (gg + 1) * HD], src[:],
                             start=(u == 0 and kc == 0), stop=True, skip_group_check=True)
                ins.then_inc(pv_done, 1)
                return ins

            pe.wait_ge(const_in, 16)
            pe.wait_ge(consts_ready, 4)
            with pe.Fori(0, DEPTH) as l:
                norm_T(l, 0)
                for c in range(4):
                    pe.wait_ge(w_lo[c % 2], l * PER_LAYER_SPLITS + (c // 2 + 1))
                    wh, wl = weights(c % 2, ZW)
                    if c >= 2:
                        pe.wait_ge(z_act, l * 4 + (c - 1))
                        pe.wait_ge(z_dve, l * 4 + (c - 1))
                    for t in range(NT):
                        for k in range(KD):
                            if c == 0 and t == 0 and k % 2 == 0:
                                pe.wait_ge(n_lo, l * 16 + (k // 2 + 1))
                            tok = slice(t * P, (t + 1) * P)
                            ins = product(bank(4 + 2 * (c % 2) + t)[:, 0:ZW], hiA[:, k, tok], loA[:, k, tok], wh[:, k, :], wl[:, k, :],
                                          k == 0, k == KD - 1)
                        ins.then_inc(z_done, 1)
                norm_T(l, 1)
                pe.wait_ge(rope_done, l + 1)
                pe.wait_ge(z_act, l * 4 + 4)
                pe.wait_ge(z_dve, l * 4 + 4)
                for b in range(3):
                    for c in (2 * b, 2 * b + 1):
                        for t in range(NT):
                            ins = nc.tensor.transpose(bank(4 + b)[:, (c % 2) * 256 + t * P:(c % 2) * 256 + (t + 1) * P],
                                                      qk_rot[:, t, c * P:(c + 1) * P], ident)
                    ins.then_inc(tq_done, 1)
                for kv in range(2):
                    for g in range(2):
                        for t in range(NT):
                            for par in range(2):
                                col = kv * 256 + g * 128 + t * 64
                                ins = mm(bank(7)[par * 64:par * 64 + 64, col:col + 64],
                                         z[:, t, Z_KCMP + kv * 128 + g * 64:Z_KCMP + kv * 128 + g * 64 + 64],
                                         ident[:, par::2], start=True, stop=True)
                ins.then_inc(xt_done, 1)
                pe.wait_ge(n_lo, l * 16 + 8)
                pe.wait_ge(n_hi, l * 16 + 8)
                for b in range(2):
                    for c in (2 * b, 2 * b + 1):
                        for t in range(NT):
                            ins = nc.tensor.transpose(bank(b)[:, (c % 2) * 256 + t * P:(c % 2) * 256 + (t + 1) * P],
                                                      z[:, t, c * P:(c + 1) * P], ident)
                    ins.then_inc(tr_done, 1)
                for g in range(4):
                    out = bank(2 + g // 2)[:, (g % 2) * 256:(g % 2) * 256 + 256]
                    u0 = Z_U + g * P
                    mm(out, z[:, 0, u0:u0 + P], cst("band", g * 384, g * 384 + 256), start=True, stop=False, skip_group_check=True)
                    ins = mm(out[:, P:256], z[:, 1, u0:u0 + P], cst("band", g * 384 + 256, (g + 1) * 384), start=False, stop=True,
                             skip_group_check=True)
                    if g % 2:
                        ins.then_inc(pd_done, 1)
                pe.wait_ge(q_rot_ready, l * 3 + 3)
                pe.wait_ge(q_raw_ready, l * 2 + 2)
                pe.wait_ge(d_ready, l * 2 + 2)
                scores(l, 0, 0, 1)
                for kv in range(2):
                    pe.wait_ge(blk_ready, l * 2 + (kv + 1))
                    pe.wait_ge(w_in_ring[kv], (l * PER_LAYER_LOADS + 3) * 16)
                    w1 = stage[kv][:].rearrange("p (j n) -> p j n", j=CMP_J)
                    for j in range(CMP_J):
                        ins = mm(bank(6 + kv)[0:2 * N_CMP, 0:256], blk_T[:, kv, j, :], w1[:, j, :],
                                 start=(j == 0), stop=(j == CMP_J - 1))
                    ins.then_inc(hid_done, 1)
                for g in range(4):
                    ins = mm(bank(4 + g // 2)[:, (g % 2) * 256:(g % 2) * 256 + 256], sml("w_pool", g * P, (g + 1) * P), d_T[:, g, :],
                             start=True, stop=True)
                    if g % 2:
                        ins.then_inc(y_done, 1)
                pe.wait_ge(hid_copied, l * 2 + 2)
                for g in range(4):
                    ins = nc.tensor.transpose(bank(6)[:, g * P:(g + 1) * P], z[:, 0, g * P:(g + 1) * P], ident)
                ins.then_inc(hidT_done, 1)
                pe.wait_ge(exps_done, l * 4 + 1)
                scores(l, 1, 1, 1)
                pe.wait_ge(gelu_done, l + 1)
                for g in range(2):
                    for hc in range(2):
                        mm(bank(7)[g * HD:(g + 1) * HD, 0:N_CMP], sml("w2k", hc * HD, (hc + 1) * HD),
                           hid[:, 0, hc, g * N_CMP:(g + 1) * N_CMP], start=(hc == 0), stop=(hc == 1))
                for g in range(2):
                    for hc in range(2):
                        ins = mm(bank(7)[0:N_CMP, 64 + g * HD:64 + (g + 1) * HD], hid[:, 1, hc, g * N_CMP:(g + 1) * N_CMP],
                                 sml("w2v", hc * HD, (hc + 1) * HD), start=(hc == 0), stop=(hc == 1))
                ins.then_inc(kcvc_done, 1)
                pe.wait_ge(kcvc_ready, l + 1)
                for h in range(HEADS):
                    rows, c = head(h)
                    for t in range(NT):
                        col = (t * GRP + c) * 16
                        ins = mm(bank(6 + h // GRP)[:, col:col + N_CMP], q_raw_T[rows, c, t * P:(t + 1) * P], k_cmp_T[rows, 0:N_CMP],
                                 start=True, stop=True)
                ins.then_inc(cs_done, 1)
                pe.wait_ge(y_hi, l * 2 + 2)
                pe.wait_ge(y_lo, l * 2 + 2)
                pe.wait_ge(cmp_v, l * 8 + 2)
                for i in range(len(groups) + 1):
                    if i < len(groups):
                        if i == 2:
                            pe.wait_ge(exps_done, l * 4 + 2)
                            scores(l, 2, 0, 0)
                            scores(l, 3, 1, 0)
                        transpose_group(l, i)
                    if i >= 1:
                        pv_group(l, i - 1)
                pe.wait_ge(cc_lo, l * 2 + 2)
                for hf in range(2):
                    s = 4 + hf
                    pe.wait_ge(w_lo[hf], l * PER_LAYER_SPLITS + (s // 2 + 1))
                    wh, wl = weights(hf)
                    for t in range(NT):
                        tok = slice(t * P, (t + 1) * P)
                        for k in range(KD):
                            ins = product(bank(2 * hf + t), hiB[:, k, tok], loB[:, k, tok], wh[:, k, :], wl[:, k, :], k == 0, k == KD - 1)
                        ins.then_inc(mix_out, 1)

                def by_feature(i, s, ah, al):
                    pe.wait_ge(w_lo[s % 2], l * PER_LAYER_SPLITS + (s // 2 + 1))
                    wh, wl = weights(s % 2)
                    if i >= 2:
                        pe.wait_ge(kvq_act, l * 6 + (i - 1))
                        pe.wait_ge(kvq_dve, l * 6 + (i - 1))
                    for n in range(4):
                        if i == 1 and n == 2:
                            norm_T(l, 2)
                        out = bank(4 + 2 * (i % 2) + n // 2)[:, (n % 2) * 256:(n % 2) * 256 + 256]
                        for k in range(KD):
                            cols = slice(n * P, (n + 1) * P)
                            ins = product(out, wh[:, k, cols], wl[:, k, cols], ah[:, k, :], al[:, k, :], k == 0, k == KD - 1)
                        if n % 2:
                            ins.then_inc(kvq_done, 1)

                by_feature(0, 6, hiA, loA)
                by_feature(1, 7, hiA, loA)
                pe.wait_ge(n_lo, l * 16 + 12)
                by_feature(2, 8, hiB, loB)
                by_feature(3, 9, hiB, loB)
                pe.wait_ge(kvq_act, l * 6 + 4)
                pe.wait_ge(kvq_dve, l * 6 + 4)
                for t in range(NT):
                    for h in range(XH):
                        out = bank(2 * t + h // 2)[:, (h % 2) * 256:(h % 2) * 256 + 256]
                        for dc in range(2):
                            ins = mm(out, q_x_T[:, 2 * h + dc, t * P:(t + 1) * P], kx_T[:, 2 * h + dc, :], start=(dc == 0), stop=(dc == 1))
                    ins.then_inc(xs_done, 1)
                for hf in range(2):
                    s, i = 10 + hf, 4 + hf
                    pe.wait_ge(w_lo[hf], l * PER_LAYER_SPLITS + (s // 2 + 1))
                    wh, wl = weights(hf)
                    pe.wait_ge(kvq_act, l * 6 + (i - 1))
                    pe.wait_ge(kvq_dve, l * 6 + (i - 1))
                    for t in range(NT):
                        tok = slice(t * P, (t + 1) * P)
                        for k in range(KD):
                            ins = product(bank(4 + 2 * hf + t), hiA[:, k, tok], loA[:, k, tok], wh[:, k, :], wl[:, k, :], k == 0, k == KD - 1)
                        ins.then_inc(kvq_done, 1)
                pe.wait_ge(kvq_act, l * 6 + 6)
                pe.wait_ge(kvq_dve, l * 6 + 6)
                for t in range(NT):
                    pe.wait_ge(xp_ready, l * 2 + (t + 1))
                    for hp in range(2):
                        for m in range(2):
                            for h2 in range(2):
                                col = (m * 2 + h2) * P
                                ins = nc.tensor.transpose(bank(4 + 2 * t + hp)[:, col:col + P], p_x[:, t, 2 * hp + h2, m * P:(m + 1) * P], ident)
                        ins.then_inc(xt2_done, 1)
                pe.wait_ge(pt2_ready, l * 4 + 4)
                for h in range(XH):
                    for dc in range(2):
                        for m in range(2):
                            ins = mm(bank(h)[:, dc * 256:(dc + 1) * 256], v_x[:, m, h * 256 + dc * P:h * 256 + (dc + 1) * P], pt_x[:, m, h, :],
                                     start=(m == 0), stop=(m == 1))
                    ins.then_inc(ox_done, 1)
                for hf in range(2):
                    s = 12 + hf
                    pe.wait_ge(w_lo[hf], l * PER_LAYER_SPLITS + (s // 2 + 1))
                    wh, wl = weights(hf)
                    for t in range(NT):
                        tok = slice(t * P, (t + 1) * P)
                        for k in range(KD):
                            if hf == 0 and t == 0 and k % 2 == 0:
                                pe.wait_ge(ox_lo, l * 4 + (k // 2 + 1))
                            ins = product(bank(4 + 2 * hf + t), hiA[:, k, tok], loA[:, k, tok], wh[:, k, :], wl[:, k, :], k == 0, k == KD - 1)
                        ins.then_inc(cross_out, 1)
                norm_T(l, 3)
                pe.wait_ge(n_lo, l * 16 + 16)

                with pe.If(l < 1):
                    def wf(kind):
                        k = KD if kind < 2 else 2
                        return (whi[kind][:, 0:2048].rearrange("p (k n) -> p k n", k=k), wlo[kind][:, 0:2048].rearrange("p (k n) -> p k n", k=k))

                    def up(kind, t, first):
                        pe.wait_ge(w_lo[kind], t + (LAYER_SPLITS + 1))
                        wh, wl = wf(kind)
                        if not first:
                            pe.wait_ge(f_silu if kind == 0 else f_mul, t + 0)
                        for n in range(2):
                            for k in range(KD):
                                cols = slice(n * P, (n + 1) * P)
                                ins = product(bank(kind)[:, n * 256:(n + 1) * 256], wh[:, k, cols], wl[:, k, cols], hiB[:, k, :], loB[:, k, :],
                                              k == 0, k == KD - 1)
                        ins.then_inc(w_used[kind], 1)

                    def down(t, first=False, last=False):
                        pe.wait_ge(w_lo[2], t + 1)
                        pe.wait_ge(f_lo_s, t + 1)
                        wh, wl = wf(2)
                        for tt in range(NT):
                            tok = slice(tt * P, (tt + 1) * P)
                            for hf in range(2):
                                cols = slice(hf * 512, (hf + 1) * 512)
                                for c in range(2):
                                    ins = product(bank(4 + 2 * tt + hf), f_hi[:, c, tok], f_lo[:, c, tok], wh[:, c, cols], wl[:, c, cols],
                                                  first and c == 0, last and c == 1)
                        ins.then_inc(w_used[2], 1)

                    up(0, 0, True)
                    up(1, 0, True)
                    up(0, 1, False)
                    down(0, first=True)
                    up(1, 1, False)
                    with pe.Fori(2, FF_STEPS) as t:
                        up(0, t, False)
                        down(t - 1)
                        up(1, t, False)
                    down(FF_STEPS - 1, last=True)

            pe.wait_ge(router_parts, 2)
            for k in range(KD):
                product(bank(0)[0:E, 0:SEQ], router_hi[:, k, :], router_lo[:, k, :], hiB[:, k, :], loB[:, k, :], k == 0, False)
                ins = mm(bank(0)[0:E, 0:SEQ], router_lo[:, k, :], loB[:, k, :], start=False, stop=(k == KD - 1))
            ins.then_inc(lg_done, 1)
            pe.wait_ge(lgT_ready, 1)
            for t in range(NT):
                ins = nc.tensor.transpose(bank(1)[:, 32 + t * E:32 + (t + 1) * E], lg_T[:, t * P:(t + 1) * P], ident[0:E, 0:E])
            ins.then_inc(lg_done, 1)
            pe.wait_ge(rv, 7)
            member = rt[:, 240:256]
            below, one = cst("below"), ones[:]
            mm(bank(1)[:, 0:E], below, member[:, 0:E], start=True, stop=True)
            mm(bank(1)[:, E:2 * E], one, member[:, 0:E], start=True, stop=False)
            mm(bank(1)[:, E:2 * E], below, member[:, E:2 * E], start=False, stop=True)
            mm(bank(1)[:, 2 * E:3 * E], one, member[:, 0:E], start=True, stop=False)
            mm(bank(1)[:, 2 * E:3 * E], one, member[:, E:2 * E], start=False, stop=True).then_inc(pos_done, 1)

            def gather(it):
                pe.wait_ge(oh_ready, it + 1)
                for k in range(KD):
                    for t in range(NT):
                        out, cols = bank(6 + k // 4)[:, (k % 4) * P:(k % 4) * P + CAP], slice(k * P, (k + 1) * P)
                        mm(out, xs_hi[:, t, cols], onehot[:, t, :], start=(t == 0), stop=False)
                        ins = mm(out, xs_lo[:, t, cols], onehot[:, t, :], start=False, stop=(t == NT - 1))
                ins.then_inc(gath_done, 1)

            def turn(n):
                pe.wait_ge(m_mul, n)
                for c in range(4):
                    ins = nc.tensor.transpose(bank(4)[:, c * P:(c + 1) * P], hid_tok[:, 1, c * P:(c + 1) * P], ident)
                ins.then_inc(mt_done, 1)

            def down_e(n, start, stop):
                pe.wait_ge(w_lo[2], n + MOE_SPLITS[2])
                pe.wait_ge(ma_lo, n)
                wh = whi[2][:].rearrange("p (c n) -> p c n", c=4)
                wl = wlo[2][:].rearrange("p (c n) -> p c n", c=4)
                for hf in range(2):
                    cols = slice(hf * 512, (hf + 1) * 512)
                    for c in range(4):
                        ins = product(bank(2 + hf), a_hi[:, c * P:(c + 1) * P], a_lo[:, c * P:(c + 1) * P], wh[:, c, cols], wl[:, c, cols],
                                      start and c == 0, stop and c == 3)
                ins.then_inc(w_used[2], 1)

            def scatter(it, j):
                t, hf = divmod(j, 2)
                if j == 0:
                    pe.wait_ge(md_lo, it)
                    pe.wait_ge(ohT_ready, it)
                if j:
                    pe.wait_ge(sc_add, it * 4 + j)
                mm(bank(5), onehot_T[:, t * P:(t + 1) * P], down_hi[:, hf * 512:(hf + 1) * 512], start=True, stop=False)
                mm(bank(5), onehot_T[:, t * P:(t + 1) * P], down_lo[:, hf * 512:(hf + 1) * 512], start=False, stop=True).then_inc(sc_done, 1)

            def item(it, first=False):
                for s in range(MOE_STEPS):
                    n = it * MOE_STEPS + s
                    begin = first and s == 0
                    for kind in range(2):
                        pe.wait_ge(w_lo[kind], n + (MOE_SPLITS[kind] + 1))
                        wh, wl = weights(kind)
                        if kind == 0:
                            if s == 0:
                                pe.wait_ge(e_lo_s, it + 1)
                            if not begin:
                                pe.wait_ge(m_silu, n)
                        for k in range(KD):
                            ins = product(bank(kind), e_hi[:, k, :], e_lo[:, k, :], wh[:, k, :], wl[:, k, :], k == 0, k == KD - 1)
                        ins.then_inc(w_used[kind], 1)
                        if kind == 0 and not begin:
                            turn(n)
                    if s == MOE_STEPS - 1:
                        pe.wait_ge(ohT_ready, it + 1)
                        gather(it + 1)
                    if not begin:
                        if s == 1 and not first:
                            pe.wait_ge(md_lo, it)
                        down_e(n, s == 1, s == 0)
                    if 1 <= s <= 4 and not first:
                        scatter(it, s - 1)
                    if s == 4:
                        for t in range(NT):
                            nc.tensor.transpose(bank(6)[:, t * P:(t + 1) * P], f32(onehot[:, t, :]), ident)
                        for t in range(NT):
                            ins = mm(bank(6)[:, SEQ:SEQ + 1], f32(onehot[:, t, :]), gate_tok[:, t:t + 1], start=(t == 0), stop=(t == NT - 1))
                        ins.then_inc(ohT_done, 1)

            pe.wait_ge(xg_lo, 1)
            gather(0)
            item(0, first=True)
            pe.wait_ge(items_ready, 1)
            n_items = pe.value_load(items_i[0:1, NCOL:NCOL + 1], min_val=E, max_val=2 * E)
            with pe.Fori(1, n_items) as it:
                item(it)
            steps = n_items * MOE_STEPS
            turn(steps)
            pe.wait_ge(ma_lo, steps)
            wh, wl = whi[2][:].rearrange("p (c n) -> p c n", c=4), wlo[2][:].rearrange("p (c n) -> p c n", c=4)
            for h in range(2):
                pe.wait_ge(w_lo[2], steps + (MOE_SPLITS[2] + h))
                for hf in range(2):
                    cols = slice(hf * 512, (hf + 1) * 512)
                    for c in (2 * h, 2 * h + 1):
                        ins = product(bank(2 + hf), a_hi[:, c * P:(c + 1) * P], a_lo[:, c * P:(c + 1) * P], wh[:, c, cols], wl[:, c, cols],
                                      False, c == 3)
            ins.then_inc(w_used[2], 1)
            pe.wait_ge(md_lo, n_items)
            pe.wait_ge(ohT_ready, n_items)
            for j in range(4):
                t, hf = divmod(j, 2)
                out, sel = bank(4 + j), onehot_T[:, t * P:(t + 1) * P]
                mm(out, sel, down_hi[:, hf * 512:(hf + 1) * 512], start=True, stop=False)
                mm(out, sel, down_lo[:, hf * 512:(hf + 1) * 512], start=False, stop=True).then_inc(sc_done, 1)

        @block.vector
        def _(dve):
            V = nc.vector

            def lo(slot, fill, n=4096):
                dve.wait_ge(w_hi[slot], fill)
                V.tensor_tensor(wlo[slot][:, 0:n], stage[slot][:, 0:n], f32(whi[slot][:, 0:n]), ALU.subtract).then_inc(w_lo[slot], 1)

            def lo_layer(l, s):
                lo(s % 2, l * PER_LAYER_SPLITS + (s // 2 + 1), KD * ZW if s < 4 else 4096)

            def norm_scale(src, n):
                dve.wait_ge(ssq_done, n)
                V.tensor_scalar(stat[:, 4:6], stat[:, 0:2], 1.0 / D, EPS, ALU.mult, ALU.add).then_inc(ms_done, 1)
                dve.wait_ge(rstd_done, n)
                for t in range(NT):
                    ins = V.tensor_scalar(xs[:, t, :], src[:, t, :], stat[:, 6 + t:7 + t], None, ALU.mult)
                ins.then_inc(xs_ready, 1)

            def norm_lo(l, j, gain, hi_, lo_):
                for i in range(4):
                    dve.wait_ge(n_hi, l * 16 + (4 * j + i + 1))
                    for k in (2 * i, 2 * i + 1):
                        ins = V.scalar_tensor_tensor(out=lo_[:, k, :], in0=bank(i)[:, (k % 2) * 256:(k % 2) * 256 + 256],
                                                     scalar=sml(gain, k, k + 1), in1=f32(hi_[:, k, :]), op0=ALU.mult, op1=ALU.subtract)
                    ins.then_inc(n_lo, 1)

            def unit_max(l, u, tt, slot):
                nk = P * (tt + 1)
                b0 = 2 if u == 3 else 0
                dve.wait_ge(s_done, l * 4 + (u + 1))
                sc = PS[:, b0:b0 + HEADS * nk // 512, :].rearrange("p b (h n) -> p (b h) n", n=nk)
                nm = stat[:, 16 + 8 * slot:24 + 8 * slot]
                V.tensor_reduce(nm, sc, AX, ALU.max).then_inc(max_done, 1)
                dve.wait_ge(max_done, l * 4 + (u + 1))
                V.tensor_scalar(nm, nm, -(HD ** -0.5), None, ALU.mult).then_inc(nm_ready, 1)

            def unit_scale(l, u, br, tt, slot):
                nk = P * (tt + 1)
                dve.wait_ge(exps_done, l * 4 + (u + 1))
                r = stat[:, 32 + 8 * slot:40 + 8 * slot]
                V.reciprocal(r, r).then_inc(r_done, 1)
                dve.wait_ge(r_done, l * 8 + (2 * u + 1))
                dve.wait_ge(gate_v, l * 3 + 2)
                V.tensor_tensor(r, r, gates[:, tt, 1 + br::3], ALU.mult).then_inc(r_done, 1)
                dve.wait_ge(r_done, l * 8 + (2 * u + 2))
                pr = probs[slot][:, 0:HEADS * nk].rearrange("p (h n) -> p h n", h=HEADS)
                V.tensor_tensor(pr, pr, r.unsqueeze(2).to_broadcast([P, HEADS, nk]), ALU.mult).then_inc(p_ready, 1)

            def pt_odd(l, i):
                dve.wait_ge(t_done, l * 13 + (i + 1))
                if i >= 2:
                    dve.wait_ge(pv_done, l * 13 + (i - 1))
                V.tensor_copy(pt[1][:], bank(7)).then_inc(pt_dve, 1)

            V.memset(stat[:, 57:58], 0.0).then_inc(sc_add, 4)
            V.memset(stat[:, 58:59], 0.0).then_inc(sc_done, 4)
            V.memset(stat[:, 56:57], 0.0).then_inc(x_ready, NT)
            dve.wait_ge(const_in, 16)
            dve.wait_ge(mask_in, 16)
            V.tensor_copy(ident_bf[:], ident).then_inc(consts_ready, 1)
            V.tensor_copy(causal_bf[:], cmask_f[:]).then_inc(consts_ready, 1)
            dve.wait_ge(consts_ready, 4)
            dve.wait_ge(x_in, 16)
            with dve.Fori(0, DEPTH) as l:
                norm_scale(x, l * 4 + 1)
                lo_layer(l, 0)
                dve.wait_ge(small_in, l * 16 + 16)
                norm_lo(l, 0, "g_mix", hiA, loA)
                lo_layer(l, 1)
                for c in range(4):
                    if c == 3:
                        norm_scale(xs, l * 4 + 2)
                    dve.wait_ge(z_done, l * 8 + (2 * c + 2))
                    V.tensor_copy(z[:, 1, c * ZW:(c + 1) * ZW], bank(5 + 2 * (c % 2))[:, 0:ZW]).then_inc(z_dve, 1)
                    if c == 1:
                        dve.wait_ge(z_act, l * 4 + 2)
                        dve.wait_ge(z_dve, l * 4 + 2)
                        rot_in = z[:, :, 0:768].rearrange("p t (h d) -> p t h d", d=HD)[:, :, :, 0:ROPE]
                        for n, (dst, tab) in enumerate(((rope_c, "cos"), (rope_s, "sin"))):
                            t_ = cst(tab).rearrange("p (t r) -> p t r", t=NT).unsqueeze(2).to_broadcast([P, NT, 12, ROPE])
                            for t in range(NT):
                                ins = V.tensor_tensor(dst[:, t], rot_in[:, t], t_[:, t], ALU.mult)
                        ins.then_inc(rope_part, 1)
                    if c < 2:
                        lo_layer(l, c + 2)
                    if c == 1:
                        dve.wait_ge(rope_part, l + 1)
                        dve.wait_ge(qk_copied, l + 1)
                        q4 = qk_rot[:].rearrange("p t (h d) -> p t h d", d=HD)
                        V.tensor_tensor(q4[:, :, :, 0:8], rope_c[:, :, :, 0:8], rope_s[:, :, :, 8:16], ALU.subtract)
                        V.tensor_tensor(q4[:, :, :, 8:16], rope_c[:, :, :, 8:16], rope_s[:, :, :, 0:8], ALU.add).then_inc(rope_done, 1)
                norm_lo(l, 1, "g_mem", hiA, loA)
                dve.wait_ge(gate_e, l + 1)
                V.tensor_scalar(gates[:], gates[:], 1.0, None, ALU.add).then_inc(gate_v, 1)
                dve.wait_ge(gate_v, l * 3 + 1)
                V.reciprocal(gates[:], gates[:]).then_inc(gate_v, 1)
                dve.wait_ge(tq_done, l * 3 + 2)
                V.tensor_copy(q_rot_T[:, 2:4, :], bank(5).rearrange("p (c t) -> p c t", c=2)).then_inc(q_rot_ready, 1)
                dve.wait_ge(xt_done, l + 1)
                for kv in range(2):
                    for g in range(2):
                        src = bank(7)[:, kv * 256 + g * 128:kv * 256 + (g + 1) * 128]
                        pe_ = sml("pe", kv * CMP_J, (kv + 1) * CMP_J)
                        for half in range(2):
                            s_ = src[:, half * 8:half * 8 + 8 * N_CMP].rearrange("p (c j) -> p j c", j=8)
                            ins = V.tensor_tensor(blk_T[:, kv, half * 8:half * 8 + 8, g * N_CMP:(g + 1) * N_CMP], s_,
                                                  pe_[:, half * 8:half * 8 + 8].unsqueeze(2).to_broadcast([P, 8, N_CMP]), ALU.add)
                    ins.then_inc(blk_ready, 1)
                dve.wait_ge(tr_done, l * 2 + 2)
                V.tensor_copy(q_raw_T[:, 2:4, :], bank(1).rearrange("p (c t) -> p c t", c=2)).then_inc(q_raw_ready, 1)
                dve.wait_ge(pd_done, l * 2 + 2)
                V.tensor_copy(d_T[:, 2:4, :], bank(3).rearrange("p (c t) -> p c t", c=2)).then_inc(d_ready, 1)
                unit_max(l, 0, 1, 0)
                for i in range(2):
                    dve.wait_ge(y_hi, l * 2 + (i + 1))
                    for g in (2 * i, 2 * i + 1):
                        ins = V.scalar_tensor_tensor(out=loB[:, 4 + g, :], in0=bank(4 + i)[:, (g % 2) * 256:(g % 2) * 256 + 256],
                                                     scalar=sml("pool_scale", g, g + 1), in1=f32(hiB[:, 4 + g, :]), op0=ALU.mult, op1=ALU.subtract)
                    ins.then_inc(y_lo, 1)
                unit_scale(l, 0, 0, 1, 0)
                dve.wait_ge(kcvc_done, l + 1)
                V.tensor_copy(k_cmp_T[:, 0:N_CMP], bank(7)[:, 0:N_CMP])
                for i in range(4):
                    ins = V.tensor_copy(v_bd[32 * i:32 * i + N_CMP, :, i * HD:(i + 1) * HD],
                                        bank(7)[0:N_CMP, 64:192].rearrange("p (g d) -> p g d", g=2))
                ins.then_inc(kcvc_ready, 1)
                unit_max(l, 1, 1, 1)
                lo_layer(l, 4)
                lc = l_cmp[:, :, 0:N_CMP]
                dve.wait_ge(cs_done, l + 1)
                cm = cst("cmp_mask").rearrange("p (r c) -> p r c", c=16)[:, :, 0:N_CMP]
                for g in range(2):
                    src = bank(6 + g)[:, 0:128].rearrange("p (r c) -> p r c", c=16)[:, :, 0:N_CMP]
                    V.scalar_tensor_tensor(out=l_cmp[:, 8 * g:8 * g + 8, 0:N_CMP], in0=src, scalar=HD ** -0.5, in1=cm,
                                           op0=ALU.mult, op1=ALU.add).then_inc(cmp_v, 1)
                dve.wait_ge(cmp_v, l * 8 + 2)
                cmax = stat[:, 64:80]
                V.tensor_reduce(cmax, lc, AX, ALU.max).then_inc(cmp_v, 1)
                dve.wait_ge(cmp_v, l * 8 + 3)
                V.tensor_scalar(cmax, cmax, 1e-10 * NEG, None, ALU.max).then_inc(cmp_v, 1)
                dve.wait_ge(cmp_v, l * 8 + 4)
                V.tensor_tensor(lc, lc, cmax.unsqueeze(2).to_broadcast([P, 16, N_CMP]), ALU.subtract)
                V.memset(l_cmp[:, :, N_CMP:16], NEG).then_inc(cmp_v, 1)
                unit_scale(l, 1, 1, 1, 1)
                pt_odd(l, 1)
                dve.wait_ge(cmp_e, l + 1)
                V.tensor_reduce(cmax, lc, AX, ALU.add).then_inc(cmp_v, 1)
                dve.wait_ge(cmp_v, l * 8 + 6)
                V.tensor_scalar(cmax, cmax, 1.1754943508222875e-38, None, ALU.max).then_inc(cmp_v, 1)
                dve.wait_ge(cmp_v, l * 8 + 7)
                V.reciprocal(cmax, cmax).then_inc(cmp_v, 1)
                dve.wait_ge(cmp_v, l * 8 + 8)
                cr = cmax.rearrange("p (g t c) -> p g t c", g=2, t=NT)
                for g in range(2):
                    ins = V.tensor_tensor(cr[:, g], cr[:, g], gates[:, :, 12 * g:12 * g + 12:3], ALU.mult)
                ins.then_inc(gate_v, 1)
                dve.wait_ge(gate_v, l * 3 + 3)
                dve.wait_ge(p_cmp_zero, l + 1)
                V.tensor_tensor(p_cmp[:, :, 0:N_CMP], lc, cmax.unsqueeze(2).to_broadcast([P, 16, N_CMP]), ALU.mult).then_inc(pc_ready, 1)
                unit_max(l, 2, 0, 0)
                pt_odd(l, 3)
                unit_max(l, 3, 0, 1)
                pt_odd(l, 5)
                unit_scale(l, 2, 0, 0, 0)
                pt_odd(l, 7)
                unit_scale(l, 3, 1, 0, 1)
                pt_odd(l, 9)
                pt_odd(l, 11)
                for i, tt in enumerate((1, 0)):
                    dve.wait_ge(cc_hi, l * 2 + (i + 1))
                    tok = slice(tt * P, (tt + 1) * P)
                    V.tensor_tensor(loB[:, 0:4, tok], bank(4 + tt).rearrange("p (c t) -> p c t", c=4), f32(hiB[:, 0:4, tok]),
                                    ALU.subtract).then_inc(cc_lo, 1)

                def add(src_bank, t, hf):
                    xv = x[:, t, hf * 512:(hf + 1) * 512]
                    return V.tensor_tensor(xv, xv, bank(src_bank), ALU.add)

                lo_layer(l, 5)
                lo_layer(l, 6)
                for hf in range(2):
                    for t in range(NT):
                        dve.wait_ge(mix_out, l * 4 + (2 * hf + t + 1))
                        ins = add(2 * hf + t, t, hf)
                        if hf:
                            ins.then_inc(x_ready, 1)
                    if hf == 0:
                        lo_layer(l, 7)
                norm_scale(x, l * 4 + 3)
                dests = [kx_T[:, 2:4, :], kx_T[:, 6:8, :], q_x_T[:, 2:4, :], q_x_T[:, 6:8, :], v_x[:, 1, 0:512], v_x[:, 1, 512:1024]]

                def kvq(i):
                    dve.wait_ge(kvq_done, l * 12 + (2 * i + 2))
                    src = bank(5 + 2 * (i % 2))
                    src = src if i >= 4 else src.rearrange("p (c t) -> p c t", c=2)
                    V.tensor_copy(dests[i], src).then_inc(kvq_dve, 1)

                kvq(0)
                lo_layer(l, 8)
                norm_lo(l, 2, "g_x", hiB, loB)
                kvq(1)
                lo_layer(l, 9)
                kvq(2)
                lo_layer(l, 10)
                kvq(3)
                lo_layer(l, 11)
                for t in range(NT):
                    dve.wait_ge(xs_done, l * 2 + (t + 1))
                    sc = PS[:, 2 * t:2 * t + 2, :].rearrange("p b (h n) -> p (b h) n", n=SEQ)
                    V.tensor_reduce(stat[:, 8 + 4 * t:12 + 4 * t], sc, AX, ALU.max).then_inc(xmax_done, 1)
                    dve.wait_ge(xmax_done, l * 2 + (t + 1))
                    V.tensor_scalar(stat[:, 16 + 4 * t:20 + 4 * t], stat[:, 8 + 4 * t:12 + 4 * t], -(256 ** -0.5), None,
                                    ALU.mult).then_inc(xnm_ready, 1)
                for t in range(NT):
                    dve.wait_ge(xexp_done, l * 2 + (t + 1))
                    r = stat[:, 48 + 4 * t:52 + 4 * t]
                    V.reciprocal(r, stat[:, 32 + 4 * t:36 + 4 * t]).then_inc(xr_done, 1)
                    dve.wait_ge(xr_done, l * 2 + (t + 1))
                    V.tensor_tensor(p_x[:, t], p_x[:, t], r.unsqueeze(2).to_broadcast([P, XH, SEQ]), ALU.mult).then_inc(xp_ready, 1)
                kvq(4)
                lo_layer(l, 12)
                kvq(5)
                for t in range(NT):
                    dve.wait_ge(xt2_done, l * 4 + (2 * t + 2))
                    V.tensor_copy(pt_x[:, :, 2:4, t * P:(t + 1) * P],
                                  bank(5 + 2 * t).rearrange("p (m h t) -> p m h t", m=2, h=2)).then_inc(pt2_ready, 1)
                lo_layer(l, 13)
                for i in range(4):
                    dve.wait_ge(ox_hi, l * 4 + (i + 1))
                    V.tensor_tensor(loA[:, 2 * i:2 * i + 2, :], bank(i).rearrange("p (c t) -> p c t", c=2), f32(hiA[:, 2 * i:2 * i + 2, :]),
                                    ALU.subtract).then_inc(ox_lo, 1)
                for hf in range(2):
                    for t in range(NT):
                        dve.wait_ge(cross_out, l * 4 + (2 * hf + t + 1))
                        ins = add(4 + 2 * hf + t, t, hf)
                        if hf:
                            ins.then_inc(x_ready, 1)
                norm_scale(x, l * 4 + 4)
                norm_lo(l, 3, "g_ffn", hiB, loB)

                with dve.If(l < 1):
                    def flo(kind, t):
                        lo(kind, t + ((LAYER_SPLITS if kind < 2 else 0) + 1), 2048)

                    def dense(t, last=False):
                        if not last:
                            flo(0, t + 1)
                        flo(2, t)
                        dve.wait_ge(f_silu, t + 1)
                        dve.wait_ge(w_used[1], t + 1)
                        V.tensor_tensor(f_act[:], f_sil[:], bank(1), ALU.mult).then_inc(f_mul, 1)
                        dve.wait_ge(f_hi_s, t + 1)
                        V.tensor_tensor(f_lo[:], f_act[:].rearrange("p (c t) -> p c t", c=2), f32(f_hi[:]), ALU.subtract).then_inc(f_lo_s, 1)
                        if not last:
                            flo(1, t + 1)

                    flo(0, 0)
                    flo(1, 0)
                    with dve.Fori(0, FF_STEPS - 1) as t:
                        dense(t)
                    dense(FF_STEPS - 1, last=True)
                    dve.wait_ge(w_used[2], FF_STEPS)
                    for t in range(NT):
                        for hf in range(2):
                            ins = add(4 + 2 * t + hf, t, hf)
                        ins.then_inc(x_ready, 1)

            dve.wait_ge(router_parts, 1)
            V.tensor_tensor(router_lo[:], router[:], f32(router_hi[:]), ALU.subtract).then_inc(router_parts, 1)
            dve.wait_ge(xg_hi, 1)
            dve.wait_ge(xT_done, 16 * DEPTH)
            V.tensor_tensor(xs_lo[:], xs[:], f32(xs_hi[:]), ALU.subtract).then_inc(xg_lo, 1)
            n_rv = [0]

            def step(ins):
                ins.then_inc(rv, 1)
                n_rv[0] += 1
                dve.wait_ge(rv, n_rv[0])

            lg = rt[:, 0:16].rearrange("p (t e) -> p t e", t=NT)
            gt = rt[:, 16:144].rearrange("p (t e j) -> p t e j", t=NT, e=E)
            rank = rt[:, 144:160].rearrange("p (t e) -> p t e", t=NT)
            m0, m1 = (rt[:, a:a + 16].rearrange("p (t e) -> p t e", t=NT) for a in (160, 176))
            w0, w1_ = (rt[:, a:a + 16].rearrange("p (t e) -> p t e", t=NT) for a in (192, 208))
            member = rt[:, 240:256].rearrange("p (t e) -> p t e", t=NT)
            eq = rt[:, 384:512].rearrange("p (t e j) -> p t e j", t=NT, e=E)
            jlt = cst("jlt").rearrange("p (e j) -> p e j", e=E)
            v1, v2, dif, ex = rt[:, 256:258], rt[:, 262:264], rt[:, 258:260], rt[:, 260:262]
            V.memset(ones[:], 1.0)
            V.memset(keys[:], -1.0)
            V.memset(combs[:], 0.0)
            V.memset(items_f[:], 0.0)
            dve.wait_ge(lg_done, 1)
            V.tensor_copy(lg_T, bank(0)[0:E, 0:SEQ]).then_inc(lgT_ready, 1)
            dve.wait_ge(lg_done, 2)
            step(V.tensor_copy(lg, bank(1)[:, 32:48].rearrange("p (t e) -> p t e", t=NT)))
            for t in range(NT):
                lj = lg[:, t].unsqueeze(1).to_broadcast([P, E, E])
                le = lg[:, t].unsqueeze(2).to_broadcast([P, E, E])
                V.tensor_tensor(gt[:, t], lj, le, ALU.is_gt)
                ins = V.tensor_tensor(eq[:, t], lj, le, ALU.is_equal)
            step(ins)
            for t in range(NT):
                ins = V.tensor_tensor(eq[:, t], eq[:, t], jlt, ALU.mult)
            step(ins)
            step(V.tensor_tensor(rt[:, 16:144], rt[:, 16:144], rt[:, 384:512], ALU.add))
            step(V.tensor_reduce(rt[:, 144:160], rt[:, 16:144].rearrange("p (r j) -> p r j", j=E), AX, ALU.add))
            V.tensor_scalar(rt[:, 160:176], rt[:, 144:160], 0.0, None, ALU.is_equal)
            step(V.tensor_scalar(rt[:, 176:192], rt[:, 144:160], 1.0, None, ALU.is_equal))
            V.tensor_tensor(rt[:, 192:208], rt[:, 160:176], rt[:, 0:16], ALU.mult)
            V.tensor_tensor(rt[:, 208:224], rt[:, 176:192], rt[:, 0:16], ALU.mult)
            step(V.tensor_tensor(rt[:, 240:256], rt[:, 160:176], rt[:, 176:192], ALU.add))
            V.tensor_reduce(v1, w0, AX, ALU.add)
            step(V.tensor_reduce(v2, w1_, AX, ALU.add))
            step(V.tensor_tensor(dif, v2, v1, ALU.subtract))
            dve.wait_ge(r_exp, 1)
            gsum, g1, g2 = rt[:, 264:266], rt[:, 266:268], rt[:, 268:270]
            step(V.tensor_scalar(gsum, ex, 1.0, None, ALU.add))
            step(V.reciprocal(g1, gsum))
            step(V.tensor_tensor(g2, g1, ex, ALU.mult))
            V.tensor_tensor(w0, m0, g1.unsqueeze(2).to_broadcast([P, NT, E]), ALU.mult)
            step(V.tensor_tensor(w1_, m1, g2.unsqueeze(2).to_broadcast([P, NT, E]), ALU.mult))
            V.tensor_tensor(combs[:, :, 0:E], w0, w1_, ALU.add)
            dve.wait_ge(pos_done, 1)
            k1 = rt[:, 272:288]
            step(V.scalar_tensor_tensor(out=k1, in0=bank(1)[:, 0:16], scalar=1.0, in1=rt[:, 240:256], op0=ALU.add, op1=ALU.mult))
            step(V.tensor_scalar(keys[:, :, 0:E], k1.rearrange("p (t e) -> p t e", t=NT), -1.0, None, ALU.add))

            def onehots(it):
                for t in range(NT):
                    ins = V.tensor_scalar(onehot[:, t, :], cst("iota", 0, CAP), keys[:, t, bass.ds(it, 1)], None, ALU.is_equal)
                V.tensor_copy(gate_tok, combs[:, :, bass.ds(it, 1)].rearrange("p t o -> p (t o)")).then_inc(oh_ready, 1)

            def mlo(kind, n):
                lo(kind, n + (MOE_SPLITS[kind] + 1))

            def gathered_lo(it):
                dve.wait_ge(e_hi_s, it + 1)
                for k in range(KD):
                    ins = V.scalar_tensor_tensor(out=e_lo[:, k, :], in0=bank(6 + k // 4)[:, (k % 4) * P:(k % 4) * P + P],
                                                 scalar=sml("g_ffn", k, k + 1), in1=f32(e_hi[:, k, :]), op0=ALU.mult, op1=ALU.subtract)
                ins.then_inc(e_lo_s, 1)

            onehots(0)
            ov = rt[:, 288:296]
            V.tensor_scalar(ov, bank(1)[:, 16:24], float(CAP), None, ALU.is_gt).then_inc(rv, 1)
            n_rv[0] += 1
            mlo(0, 0)
            dve.wait_ge(rv, n_rv[0])
            mlo(1, 0)
            gathered_lo(0)
            orank = rt[:, 296:304]
            sel = rt[:, 512:576].rearrange("p (j e) -> p j e", e=E)
            tmp = rt[:, 576:640].rearrange("p (j e) -> p j e", e=E)
            iota8 = cst("iota", 0, E)
            step(V.tensor_tensor(tmp, jlt, ov.unsqueeze(1).to_broadcast([P, E, E]), ALU.mult))
            step(V.tensor_reduce(orank, tmp, AX, ALU.add))
            step(V.tensor_tensor(sel, orank.unsqueeze(1).to_broadcast([P, E, E]), iota8.unsqueeze(2).to_broadcast([P, E, E]), ALU.is_equal))
            step(V.tensor_tensor(sel, sel, ov.unsqueeze(1).to_broadcast([P, E, E]), ALU.mult))
            k2 = rt[:, 304:320].rearrange("p (t e) -> p t e", t=NT)
            step(V.tensor_scalar(k2, keys[:, :, 0:E], -float(CAP), None, ALU.add))
            for t in range(NT):
                for src, dst in ((k2[:, t], keys), (combs[:, t, 0:E], combs)):
                    step(V.tensor_tensor(tmp, sel, src.unsqueeze(1).to_broadcast([P, E, E]), ALU.mult))
                    step(V.tensor_reduce(dst[:, t, E:2 * E], tmp, AX, ALU.add))
            step(V.tensor_tensor(tmp, sel, iota8.unsqueeze(1).to_broadcast([P, E, E]), ALU.mult))
            V.tensor_reduce(items_f[:, E:2 * E], tmp, AX, ALU.add)
            V.tensor_copy(items_f[:, 0:E], iota8)
            step(V.tensor_reduce(rt[:, 320:321], ov, AX, ALU.add))
            step(V.tensor_scalar(items_f[:, NCOL:NCOL + 1], rt[:, 320:321], float(E), None, ALU.add))
            V.tensor_copy(items_i[:], items_f[:]).then_inc(items_ready, 1)

            def multiply(n):
                dve.wait_ge(m_silu, n)
                dve.wait_ge(w_used[1], n + FF_STEPS)
                V.tensor_tensor(hid_tok[:, 1, :], hid_tok[:, 0, :], bank(1), ALU.mult).then_inc(m_mul, 1)

            def act_lo(n):
                dve.wait_ge(ma_hi, n)
                V.tensor_tensor(a_lo[:], bank(4), f32(a_hi[:]), ALU.subtract).then_inc(ma_lo, 1)

            def scatter_add(it, j):
                t, hf = divmod(j, 2)
                dve.wait_ge(sc_done, it * 4 + (j + 1))
                xv = x[:, t, hf * 512:(hf + 1) * 512]
                return V.tensor_tensor(xv, xv, bank(5), ALU.add).then_inc(sc_add, 1)

            def down_parts(it):
                dve.wait_ge(md_hi, it)
                V.scalar_tensor_tensor(out=down_lo[:].rearrange("p (b n) -> p b n", b=2), in0=PS[:, 2:4, :], scalar=gate_slot,
                                       in1=f32(down_hi[:]).rearrange("p (b n) -> p b n", b=2), op0=ALU.mult, op1=ALU.subtract).then_inc(md_lo, 1)

            def item(it, first=False):
                for s in range(MOE_STEPS):
                    n = it * MOE_STEPS + s
                    begin = first and s == 0
                    if s == MOE_STEPS - 1:
                        dve.wait_ge(gath_done, it + 1)
                        dve.wait_ge(ohT_done, it + 1)
                        onehots(it + 1)
                    if not begin:
                        mlo(0, n)
                        if s == 0:
                            gathered_lo(it)
                        multiply(n)
                        mlo(1, n)
                    if s == 1 and not first:
                        down_parts(it)
                    if not begin:
                        mlo(2, n - 1)
                        act_lo(n)
                    if 2 <= s <= 5 and not first:
                        scatter_add(it, s - 2)

            item(0, first=True)
            n_items = dve.value_load(items_i[0:1, NCOL:NCOL + 1], min_val=E, max_val=2 * E)
            with dve.Fori(1, n_items) as it:
                item(it)
            last = n_items * MOE_STEPS
            multiply(last)
            act_lo(last)
            for h in range(2):
                dve.wait_ge(w_hi[2], last + (MOE_SPLITS[2] + h))
                half = slice(h * 2048, (h + 1) * 2048)
                V.tensor_tensor(wlo[2][:, half], stage[2][:, half], f32(whi[2][:, half]), ALU.subtract).then_inc(w_lo[2], 1)
            down_parts(n_items)
            for j in range(4):
                t, hf = divmod(j, 2)
                dve.wait_ge(sc_done, n_items * 4 + (j + 1))
                xv = x[:, t, hf * 512:(hf + 1) * 512]
                ins = V.tensor_tensor(xv, xv, bank(4 + j), ALU.add)
                if hf:
                    ins.then_inc(x_ready, 1)
            dve.wait_ge(ssq_done, DEPTH * 4 + 1)
            V.tensor_scalar(stat[:, 4:6], stat[:, 0:2], 1.0 / D, EPS, ALU.mult, ALU.add).then_inc(ms_done, 1)
            dve.wait_ge(rstd_done, DEPTH * 4 + 1)
            dve.wait_ge(gfin_in, 16)
            for t in range(NT):
                V.scalar_tensor_tensor(out=xs[:, t, :], in0=x[:, t, :], scalar=stat[:, 6 + t:7 + t], in1=gfin[:],
                                       op0=ALU.mult, op1=ALU.mult).then_inc(fin_ready, 1)


def layouts(inputs):
    a = {k: np.asarray(v) for k, v in inputs.items()}
    f = np.float32
    o1, o2, o3 = NSA_W, NSA_W + 6 * 128, NSA_W + 6 * 128 + 24
    q = np.arange(o1).reshape(2, 4, HD).transpose(1, 0, 2).ravel()
    kv = lambda i: np.arange(o1 + i * 128, o1 + (i + 1) * 128)
    cols = np.concatenate([q, kv(2), kv(4), kv(0), kv(1), kv(3), kv(5), np.arange(o2, o3), np.arange(o3, IN_W)])

    def by_cols(w, n):
        r, c = w.shape
        return w.reshape(r // P, P, c // n, n).transpose(2, 1, 0, 3).reshape(c // n, P, r // P * n)

    def by_rows(w, n):
        r, c = w.shape
        return w.reshape(r // n, n // P, P, c).transpose(0, 2, 1, 3).reshape(r // n, P, n // P * c)

    wl = np.zeros((DEPTH, 16, P, 4096), f)
    for l in range(DEPTH):
        wl[l, 0:4, :, :KD * ZW] = by_cols(a["w_in"][l][:, cols], ZW)
        w_out_rows = np.concatenate([q, np.arange(NSA_W, D)])
        wl[l, 4:5] = by_rows(a["cmp_w1_k"][l], CMP_LEN * HD)
        wl[l, 5:6] = by_rows(a["cmp_w1_v"][l], CMP_LEN * HD)
        wl[l, 6:8] = by_cols(a["w_out"][l][w_out_rows], 512)
        for i, n in ((8, "wk_x"), (10, "wq_x"), (12, "wv_x"), (14, "wo_x")):
            wl[l, i:i + 2] = by_cols(a[n][l], 512)
    wf = np.stack([by_cols(a["ffn_wg"][0], FF_STEP), by_cols(a["ffn_wu"][0], FF_STEP), by_rows(a["ffn_wd"][0], FF_STEP)], axis=1)
    wm = np.empty((E, MOE_STEPS, 3, P, 4096), f)
    for e in range(E):
        wm[e, :, 0] = by_cols(a["moe_wg"][0, e], MOE_STEP)
        wm[e, :, 1] = by_cols(a["moe_wu"][0, e], MOE_STEP)
        wm[e, :, 2] = by_rows(a["moe_wd"][0, e], MOE_STEP)
    small = np.zeros((DEPTH, P, SMALL_W), f)

    def put(n, v):
        o, w = SMALL[n]
        small[:, :, o:o + w] = v.reshape(DEPTH, P, w)

    col = lambda v, k: v.reshape(DEPTH, k, P).transpose(0, 2, 1)
    for n, s in (("g_mix", "norm_mix"), ("g_mem", "norm_mem"), ("g_x", "norm_x"), ("g_ffn", "norm_ffn")):
        put(n, col(a[s], KD))
    put("pool_scale", col(a["pool_scale"], 4))
    put("b1", np.concatenate([col(a["cmp_b1_k"], 2), col(a["cmp_b1_v"], 2)], axis=2))
    put("pe", np.concatenate([col(a["cmp_pe_k"], CMP_J), col(a["cmp_pe_v"], CMP_J)], axis=2))
    for n, s in (("w2k", "cmp_w2_k"), ("w2v", "cmp_w2_v")):
        put(n, a[s].reshape(DEPTH, 2, P, HD).transpose(0, 2, 1, 3))
    put("w_pool", a["w_pool"].transpose(0, 2, 1, 3))
    router = a["moe_router"][0].reshape(KD, P, E).transpose(1, 0, 2).reshape(P, KD * E)
    return {"x": a["x"][0], "mem": a["mem"][0], "wl": wl, "wf": wf, "wm": wm, "small": small, "const": constants(),
            "router": router, "gfin": a["norm_final"]}


def constants():
    f = np.float32
    c = np.zeros((P, CONST_W), f)

    def put(n, v):
        o, w = CONST[n]
        c[:, o:o + w] = np.broadcast_to(v, (P, w))

    r = np.arange(P)
    put("ident", np.eye(P, dtype=f))
    put("below", (r[:, None] < r[None, :]).astype(f))
    put("iota", r.astype(f))
    put("jlt", (np.arange(E)[None, :] < np.arange(E)[:, None]).astype(f).ravel())
    half = ROPE // 2
    inv = f(500000.0) ** (-np.arange(half, dtype=f) / f(half))
    ang = np.arange(SEQ, dtype=f)[:, None] * inv[None, :]
    for n, fn in (("cos", np.cos), ("sin", np.sin)):
        v = fn(ang.astype(np.float64)).astype(f)
        v = np.concatenate([v, v], axis=1).reshape(NT, P, ROPE).transpose(1, 0, 2).reshape(P, NT * ROPE)
        put(n, v)
    tok = np.arange(SEQ).reshape(NT, P)
    end = np.append(np.arange(N_CMP) * CMP_STRIDE + CMP_LEN - 1, 10 ** 6)
    m = np.where(end[None, None, :] <= tok[:, :, None], 0.0, NEG).astype(f)
    put("cmp_mask", np.broadcast_to(m.transpose(1, 0, 2)[:, :, None, :], (P, NT, GRP, 16)).reshape(P, 128))
    band = np.zeros((4, SEQ, SEQ), f)
    s = np.arange(SEQ)
    for g, w in enumerate((2, 4, 8, 16)):
        inside = (s[:, None] <= s[None, :]) & (s[:, None] > s[None, :] - w)
        band[g] = inside / np.minimum(s + 1, w)[None, :].astype(f) - np.eye(SEQ, dtype=f)
    put("band", np.concatenate([band[:, :P, :], band[:, P:, P:]], axis=2).transpose(1, 0, 2).reshape(P, 4 * 384))
    put("causal", np.concatenate([np.zeros((P, P), f), np.where(r[None, :] <= r[:, None], 0.0, NEG).astype(f)], axis=1))
    return c


def kernel(**inputs):
    import concourse.bacc as bacc
    from concourse.bass_utils import run_bass_kernel_spmd

    nc = bacc.Bacc("TRN2", target_bir_lowering=False, num_devices=1)
    arrays, args = {}, []
    for name, v in layouts(inputs).items():
        v = np.ascontiguousarray(v)
        arrays[f"{name}_dram"] = v
        args.append(nc.dram_tensor(f"{name}_dram", v.shape, mybir.dt.from_np(v.dtype), kind="ExternalInput").ap())
    args.append(nc.dram_tensor("out_dram", (SEQ, D), F32, kind="ExternalOutput").ap())
    build(nc, *args)
    r = run_bass_kernel_spmd(nc, [arrays], core_ids=[0])
    return r.results[0]["out_dram"].reshape(1, SEQ, D)
```
